# Optimizing a Trainium2 kernel written in Bass

```python
import math
import jax
import jax.numpy as jnp
from jax import lax
import numpy as np

D_MODEL = 2048
BATCH = 1
SEQ = 256
DEPTH = 1
DEC_BATCH = 1
DEC_SEQ = 32
PAST_LEN = 256

CHUNK = 64
Q_BLOCK = 128
MIX_WIDTH = D_MODEL
W_ATTN = MIX_WIDTH // 2
W_SSM = MIX_WIDTH - W_ATTN
HEAD_DIM = 128
N_HEADS = W_ATTN // HEAD_DIM
SSM_GROUP = 16
N_SSM_GROUPS = W_SSM // SSM_GROUP
SSM_STATE = 64
N_EXPERT_GROUPS = 4
EXPERTS_PER_GROUP = 8
N_EXPERTS = N_EXPERT_GROUPS * EXPERTS_PER_GROUP
TOP_K = 2
D_EXPERT = D_MODEL // 4
MOE_BLOCK = 128
PLE_DIM = 256
ALPHA = (2 * DEPTH) ** 0.25
BETA = (8 * DEPTH) ** -0.25
LN_EPS = 1e-5

kernel_name = 'hymba_sb_s5_hmoe_stream_step'

def layer_norm(x, g, b):
    xf = x.astype(jnp.float32)
    mu = jnp.mean(xf, -1, keepdims=True)
    var = jnp.mean(jnp.square(xf - mu), -1, keepdims=True)
    return ((xf - mu) * lax.rsqrt(var + LN_EPS) * g.astype(jnp.float32) + b.astype(jnp.float32)).astype(x.dtype)

def rms_norm(x, g):
    xf = x.astype(jnp.float32)
    return xf * lax.rsqrt(jnp.mean(jnp.square(xf), -1, keepdims=True) + LN_EPS) * g.astype(jnp.float32)

def sb_attend(q, k, v, q_pos, k_pos):
    z = jnp.einsum('bqhd,bkhd->bhqk', q, k, preferred_element_type=jnp.float32) * (HEAD_DIM ** -0.5)
    visible = k_pos[None, :] < q_pos[:, None]
    log_keep = jnp.where(visible, jax.nn.log_sigmoid(-z), 0.0)
    later = lax.cumsum(log_keep, axis=3, reverse=True) - log_keep
    w = jnp.where(visible, jnp.exp(jax.nn.log_sigmoid(z) + later), 0.0)
    out = jnp.einsum('bhqk,bkhd->bqhd', w.astype(v.dtype), v, preferred_element_type=jnp.float32)
    return out.astype(v.dtype)

def stick_breaking(q, k, v, q_pos, k_pos):
    bsz, tq = q.shape[0], q.shape[1]
    if tq > Q_BLOCK and tq % Q_BLOCK == 0:
        nb = tq // Q_BLOCK
        qb = jnp.moveaxis(q.reshape(bsz, nb, Q_BLOCK, N_HEADS, HEAD_DIM), 1, 0)
        pb = q_pos.reshape(nb, Q_BLOCK)
        ob = lax.map(lambda blk: sb_attend(blk[0], k, v, blk[1], k_pos), (qb, pb))
        return jnp.moveaxis(ob, 0, 1).reshape(bsz, tq, N_HEADS, HEAD_DIM)
    return sb_attend(q, k, v, q_pos, k_pos)

def _linear_combine(e1, e2):
    a1, b1 = e1
    a2, b2 = e2
    return a1 * a2, a2 * b1 + b2

def s5_ssm(u, h0_re, h0_im, lam_re, lam_im, log_step, b_re, b_im, c_re, c_im, d_skip, w_glu, b_glu):
    f32 = jnp.float32
    bsz, L, _ = u.shape
    uf = u.astype(f32).reshape(bsz, L, N_SSM_GROUPS, SSM_GROUP)
    lam = lax.complex(jnp.minimum(lam_re.astype(f32), -1e-4), lam_im.astype(f32))
    step = jnp.exp(log_step.astype(f32))[:, None]
    lam_bar = jnp.exp(lam * step)
    b_bar = ((lam_bar - 1.0) / lam)[:, :, None] * lax.complex(b_re.astype(f32), b_im.astype(f32))
    bu = jnp.einsum('blgc,gpc->blgp', uf.astype(jnp.complex64), b_bar)
    if h0_re is not None:
        h0 = lax.complex(h0_re.astype(f32), h0_im.astype(f32))
        bu = bu.at[:, 0].add(lam_bar * h0)
    a = jnp.broadcast_to(lam_bar, bu.shape)
    _, h = lax.associative_scan(_linear_combine, (a, bu), axis=1)
    c = lax.complex(c_re.astype(f32), c_im.astype(f32))
    y = jnp.einsum('blgp,gcp->blgc', h, c).real + d_skip.astype(f32) * uf
    z = jax.nn.gelu(y.reshape(bsz, L, W_SSM))
    out = z * jax.nn.sigmoid(z @ w_glu.astype(f32) + b_glu.astype(f32))
    return out.astype(u.dtype), h[:, -1].real, h[:, -1].imag

def expert_dispatch(x, expert_ids, gates, w_gate, w_up, w_down):
    T, D = x.shape
    A = expert_ids.shape[0]
    token_ids = jnp.arange(A, dtype=jnp.int32) // TOP_K
    order = jnp.argsort(expert_ids)
    sorted_e = expert_ids[order]
    counts = jnp.bincount(expert_ids, length=N_EXPERTS).astype(jnp.int32)
    padded = (counts + MOE_BLOCK - 1) // MOE_BLOCK * MOE_BLOCK
    start = jnp.cumsum(counts) - counts
    pad_end = jnp.cumsum(padded)
    pad_start = pad_end - padded
    dest = pad_start[sorted_e] + (jnp.arange(A, dtype=jnp.int32) - start[sorted_e])
    nb = (A + MOE_BLOCK - 1) // MOE_BLOCK + N_EXPERTS
    slot_tok = jnp.full((nb * MOE_BLOCK,), T, jnp.int32).at[dest].set(token_ids[order])
    slot_gate = jnp.zeros((nb * MOE_BLOCK,), jnp.float32).at[dest].set(gates[order].astype(jnp.float32))
    block_e = jnp.minimum(jnp.searchsorted(pad_end, jnp.arange(nb, dtype=jnp.int32) * MOE_BLOCK, side='right'), N_EXPERTS - 1)
    xpad = jnp.concatenate([x, jnp.zeros((1, D), x.dtype)], axis=0)
    xb = xpad[slot_tok].reshape(nb, MOE_BLOCK, D)

    def expert_block(args):
        xi, e = args
        hid = jax.nn.silu(xi @ w_gate[e]) * (xi @ w_up[e])
        return hid @ w_down[e]

    yb = lax.map(expert_block, (xb, block_e))
    y = jnp.zeros((T + 1, D), jnp.float32).at[slot_tok].add(yb.reshape(-1, D).astype(jnp.float32) * slot_gate[:, None])
    return y[:T].astype(x.dtype)

def hier_moe(h, w_rg, b_rg, w_re, b_re, w_gate, w_up, w_down):
    bsz, L, D = h.shape
    x = h.reshape(-1, D)
    T = x.shape[0]
    pg = jax.nn.softmax((x @ w_rg + b_rg).astype(jnp.float32), axis=-1)
    pg_top, g_idx = lax.top_k(pg, 1)
    le = (x @ w_re + b_re).astype(jnp.float32).reshape(T, N_EXPERT_GROUPS, EXPERTS_PER_GROUP)
    le_sel = le[jnp.arange(T), g_idx[:, 0]]
    pe_top, e_idx = lax.top_k(jax.nn.softmax(le_sel, axis=-1), TOP_K)
    gates = pg_top * pe_top / jnp.sum(pe_top, -1, keepdims=True)
    experts = g_idx * EXPERTS_PER_GROUP + e_idx
    y = expert_dispatch(x, experts.reshape(-1).astype(jnp.int32), gates.reshape(-1), w_gate, w_up, w_down)
    return y.reshape(bsz, L, D)

def trunk_layer(x, p, k_cache, v_cache, h0_re, h0_im, lw):
    bsz, L, _ = x.shape
    proj = x @ lw['w_in']
    q = proj[..., :W_ATTN].reshape(bsz, L, N_HEADS, HEAD_DIM)
    k = proj[..., W_ATTN:2 * W_ATTN].reshape(bsz, L, N_HEADS, HEAD_DIM)
    v = proj[..., 2 * W_ATTN:3 * W_ATTN].reshape(bsz, L, N_HEADS, HEAD_DIM)
    u = proj[..., 3 * W_ATTN:]
    if k_cache is None:
        past, k_all, v_all = 0, k, v
    else:
        past = k_cache.shape[1]
        k_all = jnp.concatenate([k_cache.astype(k.dtype), k], axis=1)
        v_all = jnp.concatenate([v_cache.astype(v.dtype), v], axis=1)
    q_pos = past + jnp.arange(L, dtype=jnp.int32)
    k_pos = jnp.arange(past + L, dtype=jnp.int32)
    attn = stick_breaking(q, k_all, v_all, q_pos, k_pos).reshape(bsz, L, W_ATTN)
    ssm, h_re, h_im = s5_ssm(u, h0_re, h0_im, lw['ssm_lam_re'], lw['ssm_lam_im'], lw['ssm_log_step'],
                             lw['ssm_b_re'], lw['ssm_b_im'], lw['ssm_c_re'], lw['ssm_c_im'], lw['ssm_d'],
                             lw['ssm_w_glu'], lw['ssm_b_glu'])
    merged = jnp.concatenate([rms_norm(attn, lw['g_attn']), rms_norm(ssm, lw['g_ssm'])], axis=-1).astype(x.dtype)
    h = layer_norm(ALPHA * x + merged @ lw['w_out'], lw['ln1_g'], lw['ln1_b'])
    moe = hier_moe(h, lw['router_w_group'], lw['router_b_group'], lw['router_w_expert'], lw['router_b_expert'],
                   lw['exp_w_gate'], lw['exp_w_up'], lw['exp_w_down'])
    ple = jax.nn.sigmoid(h @ lw['ple_w_gate']) * (p.astype(h.dtype) @ lw['ple_w_proj'])
    x_new = layer_norm(ALPHA * h + moe + ple, lw['ln2_g'], lw['ln2_b'])
    return x_new, k, v, h_re, h_im

def setup_inputs(seed: int = 0) -> dict:
    key = jax.random.key(seed)
    kit = iter([jax.random.fold_in(key, i) for i in range(48)])
    f32 = jnp.float32

    def nrm(shape, scale):
        return jax.random.normal(next(kit), shape, f32) * scale

    def gain(shape):
        return 1.0 + nrm(shape, 0.01)

    D = D_MODEL
    col_scale = jnp.concatenate([jnp.ones((2 * W_ATTN,), f32), jnp.full((W_ATTN,), BETA, f32), jnp.ones((W_SSM,), f32)])
    lam_im = jnp.broadcast_to(jnp.pi * jnp.arange(SSM_STATE, dtype=f32), (DEPTH, N_SSM_GROUPS, SSM_STATE))
    return {
        'x_prompt': nrm((BATCH, SEQ, D), 1.0),
        'x_sample': nrm((DEC_BATCH, DEC_SEQ, D), 1.0),
        'p_prompt': nrm((DEPTH, BATCH, SEQ, PLE_DIM), 1.0),
        'p_sample': nrm((DEPTH, DEC_BATCH, DEC_SEQ, PLE_DIM), 1.0),
        'cache_k': nrm((DEPTH, DEC_BATCH, PAST_LEN, N_HEADS, HEAD_DIM), 1.0),
        'cache_v': nrm((DEPTH, DEC_BATCH, PAST_LEN, N_HEADS, HEAD_DIM), BETA),
        'state_ssm_re': nrm((DEPTH, DEC_BATCH, N_SSM_GROUPS, SSM_STATE), 0.1),
        'state_ssm_im': nrm((DEPTH, DEC_BATCH, N_SSM_GROUPS, SSM_STATE), 0.1),
        'ln_in_g': gain((D,)),
        'ln_in_b': nrm((D,), 0.01),
        'w_in': nrm((DEPTH, D, 3 * W_ATTN + W_SSM), D ** -0.5) * col_scale,
        'ssm_lam_re': -0.5 + nrm((DEPTH, N_SSM_GROUPS, SSM_STATE), 0.01),
        'ssm_lam_im': lam_im + nrm((DEPTH, N_SSM_GROUPS, SSM_STATE), 0.01),
        'ssm_log_step': jax.random.uniform(next(kit), (DEPTH, N_SSM_GROUPS), f32, math.log(1e-3), math.log(1e-1)),
        'ssm_b_re': nrm((DEPTH, N_SSM_GROUPS, SSM_STATE, SSM_GROUP), (2 * SSM_GROUP) ** -0.5),
        'ssm_b_im': nrm((DEPTH, N_SSM_GROUPS, SSM_STATE, SSM_GROUP), (2 * SSM_GROUP) ** -0.5),
        'ssm_c_re': nrm((DEPTH, N_SSM_GROUPS, SSM_GROUP, SSM_STATE), (2 * SSM_STATE) ** -0.5),
        'ssm_c_im': nrm((DEPTH, N_SSM_GROUPS, SSM_GROUP, SSM_STATE), (2 * SSM_STATE) ** -0.5),
        'ssm_d': nrm((DEPTH, N_SSM_GROUPS, SSM_GROUP), 1.0),
        'ssm_w_glu': nrm((DEPTH, W_SSM, W_SSM), W_SSM ** -0.5),
        'ssm_b_glu': nrm((DEPTH, W_SSM), 0.01),
        'g_attn': gain((DEPTH, W_ATTN)),
        'g_ssm': gain((DEPTH, W_SSM)),
        'w_out': nrm((DEPTH, MIX_WIDTH, D), BETA * MIX_WIDTH ** -0.5),
        'ln1_g': gain((DEPTH, D)),
        'ln1_b': nrm((DEPTH, D), 0.01),
        'w_router_group': nrm((DEPTH, D, N_EXPERT_GROUPS), D ** -0.5),
        'b_router_group': nrm((DEPTH, N_EXPERT_GROUPS), 0.01),
        'w_router_expert': nrm((DEPTH, D, N_EXPERTS), D ** -0.5),
        'b_router_expert': nrm((DEPTH, N_EXPERTS), 0.01),
        'w_exp_gate': nrm((DEPTH, N_EXPERTS, D, D_EXPERT), D ** -0.5),
        'w_exp_up': nrm((DEPTH, N_EXPERTS, D, D_EXPERT), D ** -0.5),
        'w_exp_down': nrm((DEPTH, N_EXPERTS, D_EXPERT, D), BETA * D_EXPERT ** -0.5),
        'w_ple_gate': nrm((DEPTH, D, D), D ** -0.5),
        'w_ple_proj': nrm((DEPTH, PLE_DIM, D), BETA * PLE_DIM ** -0.5),
        'ln2_g': gain((DEPTH, D)),
        'ln2_b': nrm((DEPTH, D), 0.01),
    }

def reference(x_prompt, x_sample, p_prompt, p_sample, cache_k, cache_v, state_ssm_re, state_ssm_im,
              ln_in_g, ln_in_b, w_in, ssm_lam_re, ssm_lam_im, ssm_log_step, ssm_b_re, ssm_b_im,
              ssm_c_re, ssm_c_im, ssm_d, ssm_w_glu, ssm_b_glu, g_attn, g_ssm, w_out, ln1_g, ln1_b,
              w_router_group, b_router_group, w_router_expert, b_router_expert,
              w_exp_gate, w_exp_up, w_exp_down, w_ple_gate, w_ple_proj, ln2_g, ln2_b):
    xp = layer_norm(x_prompt, ln_in_g, ln_in_b)
    xs = layer_norm(x_sample, ln_in_g, ln_in_b)
    kp_l, vp_l, hrp_l, hip_l = [], [], [], []
    ks_l, vs_l, hrs_l, his_l = [], [], [], []
    for l in range(DEPTH):
        lw = {
            'w_in': w_in[l],
            'ssm_lam_re': ssm_lam_re[l], 'ssm_lam_im': ssm_lam_im[l], 'ssm_log_step': ssm_log_step[l],
            'ssm_b_re': ssm_b_re[l], 'ssm_b_im': ssm_b_im[l], 'ssm_c_re': ssm_c_re[l], 'ssm_c_im': ssm_c_im[l],
            'ssm_d': ssm_d[l], 'ssm_w_glu': ssm_w_glu[l], 'ssm_b_glu': ssm_b_glu[l],
            'g_attn': g_attn[l], 'g_ssm': g_ssm[l], 'w_out': w_out[l], 'ln1_g': ln1_g[l], 'ln1_b': ln1_b[l],
            'router_w_group': w_router_group[l], 'router_b_group': b_router_group[l],
            'router_w_expert': w_router_expert[l], 'router_b_expert': b_router_expert[l],
            'exp_w_gate': w_exp_gate[l], 'exp_w_up': w_exp_up[l], 'exp_w_down': w_exp_down[l],
            'ple_w_gate': w_ple_gate[l], 'ple_w_proj': w_ple_proj[l], 'ln2_g': ln2_g[l], 'ln2_b': ln2_b[l],
        }
        xp, kp, vp, hrp, hip = trunk_layer(xp, p_prompt[l], None, None, None, None, lw)
        xs, ks, vs, hrs, his = trunk_layer(xs, p_sample[l], cache_k[l], cache_v[l], state_ssm_re[l], state_ssm_im[l], lw)
        kp_l.append(kp); vp_l.append(vp); hrp_l.append(hrp); hip_l.append(hip)
        ks_l.append(ks); vs_l.append(vs); hrs_l.append(hrs); his_l.append(his)
    k_prompt = jnp.stack(kp_l)
    v_prompt = jnp.stack(vp_l)
    ssm_re_prompt = jnp.stack(hrp_l)
    ssm_im_prompt = jnp.stack(hip_l)
    k_sample = jnp.stack(ks_l)
    v_sample = jnp.stack(vs_l)
    ssm_re_sample = jnp.stack(hrs_l)
    ssm_im_sample = jnp.stack(his_l)
    return (xp, xs, k_prompt, v_prompt, ssm_re_prompt, ssm_im_prompt, k_sample, v_sample, ssm_re_sample, ssm_im_sample)


_drawn_inputs = setup_inputs


def setup_inputs(seed=0):
    import zlib

    import numpy as np

    out = dict(_drawn_inputs(seed))
    spreads = {}
    factors = {'ln_in_g': 3.275,
     'ln_in_b': 2.846,
     'ssm_lam_re': 4.333,
     'ssm_b_glu': 8.0,
     'g_attn': 6.698,
     'g_ssm': 8.0,
     'ln1_g': 3.199,
     'ln1_b': 3.681,
     'b_router_group': 5.819,
     'b_router_expert': 3.969,
     'ln2_g': 5.801,
     'ln2_b': 5.668}
    for name, (base, spread) in spreads.items():
        noise = np.random.default_rng([zlib.crc32(name.encode()), seed]).standard_normal(out[name].shape)
        drawn = base * np.exp(spread * noise) if base else spread * noise
        out[name] = jnp.asarray(drawn.astype(out[name].dtype))
    for name, factor in factors.items():
        out[name] = (out[name] * factor).astype(out[name].dtype)
    return out
```

```python
import math
from contextlib import ExitStack

import concourse.bass as bass
from concourse import mybir

P = 128
POOL_PER_PAIR = 84
DVE_PER_CHUNK = 47
F32 = mybir.dt.float32
I32 = mybir.dt.int32
ALU = mybir.AluOpType
ACT = mybir.ActivationFunctionType
AX_X = mybir.AxisListType.X
ds = bass.ds


class OwnOrder:

    def __init__(self, eng, sem):
        self.eng, self.sem, self.base, self.n = eng, sem, 0, 0

    def __call__(self, ins):
        self.n += 1
        return ins.then_inc(self.sem, 1)

    def wait(self):
        self.eng.wait_ge(self.sem, self.base + self.n)

    def enter(self, base):
        self.base, self.n = base, 0


def build(nc, x_prompt, x_sample, p_prompt, p_sample, cache_k, cache_v, state_ssm_re, state_ssm_im,
          ln_in_g, ln_in_b, w_in, ssm_lam_re, ssm_lam_im, ssm_log_step, ssm_b_re, ssm_b_im,
          ssm_c_re, ssm_c_im, ssm_d, ssm_w_glu, ssm_b_glu, g_attn, g_ssm, w_out, ln1_g, ln1_b,
          w_router_group, b_router_group, w_router_expert, b_router_expert,
          w_exp_gate, w_exp_up, w_exp_down, w_ple_gate, w_ple_proj, ln2_g, ln2_b,
          y_prompt, y_sample, k_prompt, v_prompt, ssm_re_prompt, ssm_im_prompt,
          k_sample, v_sample, ssm_re_sample, ssm_im_sample):
    _, TP, D = x_prompt.shape
    TS = x_sample.shape[1]
    T = TP + TS
    KC = D // P
    NH, DH = cache_k.shape[3], cache_k.shape[4]
    PAST = cache_k.shape[2]
    W = NH * DH
    NCH = W // P
    NG, NS = ssm_lam_re.shape[1:]
    GC = ssm_d.shape[2]
    NJ = NG * NS // P
    JC = NJ // NCH
    NE, _, FE = w_exp_gate.shape[1:]
    NGRP = w_router_group.shape[2]
    EPG = NE // NGRP
    FC = FE // P
    PLC = w_ple_proj.shape[1] // P
    LN_EPS = 1e-5
    ALPHA = 2.0 ** 0.25
    SCALE = float(DH) ** -0.5
    NEG = -1e30
    TT = [(0, P), (P, P), (2 * P, TS)]
    NT = len(TT)
    assert (TP, TS, PAST, DH, JC, P // NS) == (256, 32, 256, P, 4, 2)
    B = 64
    MB = -(-T // B)
    NOV = T * 2 // B
    XROWS = 2 * T + B
    YROWS = (NE + NOV) * B
    RW = NGRP + NE

    x_src = [x_prompt[0, 0:P, :], x_prompt[0, P:2 * P, :], x_sample[0]]
    y_dst = [y_prompt[0, 0:P, :], y_prompt[0, P:2 * P, :], y_sample[0]]
    p_src = [p_prompt[0, 0, 0:P, :], p_prompt[0, 0, P:2 * P, :], p_sample[0, 0]]
    w_in_v = w_in[0].rearrange("(k p) n -> p k n", p=P)
    w_glu_v = ssm_w_glu[0].rearrange("(k p) n -> p k n", p=P)
    w_out_v = w_out[0].rearrange("(k p) n -> p k n", p=P)
    w_plg_v = w_ple_gate[0].rearrange("(k p) n -> p k n", p=P)
    w_plp_v = w_ple_proj[0].rearrange("(k p) n -> p k n", p=P)
    ck_v = cache_k[0, 0].rearrange("(t p) h d -> p t h d", p=P)
    cv_v = cache_v[0, 0].rearrange("(t p) h d -> p t h d", p=P)
    kp_v = k_prompt[0, 0].rearrange("(t p) h d -> p t h d", p=P)
    vp_v = v_prompt[0, 0].rearrange("(t p) h d -> p t h d", p=P)
    b_v = [b[0].rearrange("g s n -> (g s) n").rearrange("(c j p) n -> p c j n", j=JC, p=P)
           for b in (ssm_b_re, ssm_b_im)]
    c_v = [c[0].rearrange("g n s -> (g n) s").rearrange("(c p) s -> p c s", p=P) for c in (ssm_c_re, ssm_c_im)]
    rows_v = [a.rearrange("g s -> (g s)").rearrange("(j p) -> j p", p=P)
              for a in (ssm_lam_re[0], ssm_lam_im[0], state_ssm_re[0, 0], state_ssm_im[0, 0])]
    step_v = ssm_log_step[0].rearrange("(j a) -> j a", a=2)
    last_v = [a[0, 0].rearrange("g s -> (g s)").rearrange("(j p) -> j p", p=P)
              for a in (ssm_re_prompt, ssm_re_sample, ssm_im_prompt, ssm_im_sample)]
    wg_v = w_exp_gate[0].rearrange("e (k p) f -> p e k f", p=P)
    wu_v = w_exp_up[0].rearrange("e (k p) f -> p e k f", p=P)
    wd_v = w_exp_down[0].rearrange("e (j p) n -> p e j n", p=P)
    xs_dram = nc.dram_tensor("rows_by_expert", (XROWS, D), F32, kind="Internal").ap()
    ys_dram = nc.dram_tensor("expert_rows_out", (YROWS, D), F32, kind="Internal").ap()

    vec_list = [("ln_in_g", ln_in_g, KC), ("ln_in_b", ln_in_b, KC), ("g_attn", g_attn[0], NCH),
                ("g_ssm", g_ssm[0], NCH), ("b_glu", ssm_b_glu[0], NCH),
                ("ssm_d", ssm_d[0].rearrange("g n -> (g n)"), NCH)]
    vec_at, nvec = {}, 0
    for name, _, n in vec_list:
        vec_at[name] = nvec
        nvec += n

    with ExitStack() as ctx:
        def sb(name, shape, dt=F32):
            return ctx.enter_context(nc.sbuf_tensor(name, shape, dt))

        def sem(name):
            return ctx.enter_context(nc.semaphore(name))

        bank = ctx.enter_context(nc.psum_tensor("bank", [P, 8, 512], F32))

        xT = sb("xT", [P, KC, T])
        accT = xT
        hT = sb("hT", [P, KC, T])
        mergedT = hT
        w_ring = sb("w_ring", [P, 4, D])
        NEW = 3 * FE * D // (P * D)
        e_ring = sb("e_ring", [P, NEW, D])
        rows = sb("rows", [P, NT, D])
        DH2, FH = D // 2, FE // 2
        x_exp = rows[:, 0, 0:DH2]
        y_exp = rows[:, 1, 0:DH2]
        xT_exp = sb("xT_exp", [P, KC // 2, 2, B])
        hid = sb("hid", [P, FH])
        sig_exp = sb("sig_exp", [P, FH])
        hidT = sb("hidT", [P, FC // 2, 2, B])
        ident = sb("ident", [P, P])
        ones = sb("ones", [P, P])
        upper = sb("upper", [P, P])
        neg_half = sb("neg_half", [P, 1])
        zero_col = sb("zero_col", [P, 1])
        vecT = sb("vecT", [P, nvec])
        pT = sb("pT", [P, PLC, T])
        ple_sig = sb("ple_sig", [P, T])
        ple_tmp = sb("ple_tmp", [P, T])
        w_router = sb("w_router", [P, KC, RW])
        b_router = sb("b_router", [P, RW])
        stats = sb("stats", [P, NT, 4, 6])
        mean_var = sb("mean_var", [P, NT, 2])
        var_eps = sb("var_eps", [P, NT])
        rstd = sb("rstd", [P, NT])
        neg_mean = sb("neg_mean", [P, NT])
        idx = sb("idx", [P, 4, NT], I32)
        gate1 = sb("gate1", [P, NT])
        gate2 = sb("gate2", [P, NT])
        NTAB = NE + NOV + 2
        tab_f = sb("tab_f", [1, NTAB + NOV + 1])
        tab = sb("tab", [1, NTAB + NOV + 1], I32)
        flag = sb("flag", [1, 2])

        used = [0]
        e_flat = e_ring[:].rearrange("p s n -> p (s n)")
        m_flat = rows[:].rearrange("p s n -> p (s n)")

        def carve(flat, shape, cursor):
            n = int(math.prod(shape))
            v = flat[:, cursor[0]:cursor[0] + n]
            cursor[0] += n
            assert cursor[0] <= flat.shape[1], cursor
            if len(shape) == 1:
                return v
            names = "abcde"[:len(shape)]
            return v.rearrange(f"p ({' '.join(names)}) -> p {' '.join(names)}",
                               **{names[i]: shape[i] for i in range(1, len(shape))})

        def early(*shape):
            return carve(e_flat, shape, used)

        attnT = early(NCH, T)
        zT = early(NCH, T)
        uT = early(T)
        du = early(T)
        yT = early(T)
        y2 = early(T)
        ysig = early(T)
        tmp1 = early(2, T)
        tmp2 = early(2, T)
        rot = early(2, T)
        scan = early(2, T)
        h_ssm = early(2, 2, T)
        bn = early(2, JC, 2, GC)
        cn = early(2, 2, NS)
        bcT = early(4, P)
        bf = early(2, JC, GC)
        cf = early(2, NS)
        bt = early(4, JC, 2, GC)
        qT = early(T)
        kT = early(T)
        vT = early(T)
        ckT = early(PAST)
        ck = early(2, P)
        cv = early(2, P)
        k_nat = early(NT, P)
        v_nat = early(NT, P)
        ZW = P + TP + PAST + TS
        Z1, Z2 = P, P + TP
        zm = early(ZW)
        sig = early(ZW)
        keep = early(ZW)
        later = early(ZW + 3)
        wgt = early(ZW)
        wT = early(480)
        mask = early(P + TP)
        mask_s = early(PAST + TS)
        par_c = early(7, JC)
        d_c = early(1)
        last = early(2, 2, NJ)
        last_rows = early(4, P)
        sg = early(2, T)
        rms_a = early(T)
        rms_s = early(T)
        par = sb("par", [P, 7, NJ])
        coef = sb("coef", [P, 2, NJ, 2])
        par_b = sb("par_b", [P, 2])
        par_cg = sb("par_cg", [P, 2])
        g8 = sb("g8", [P, P // GC])
        io = sb("io", [P, NE])
        route_at, rank_at, place_at = [0], [0], [0]

        def route(*shape):
            return carve(xT_exp[:].rearrange("p k h n -> p (k h n)"), shape, route_at)

        logits = route(NT, RW)
        d5 = route(NT, NGRP + 1)
        e5 = route(NT, NGRP + 1)
        r_max = route(NT)
        r_low = route(NT)
        g_hot = route(NT, NGRP)
        el = route(NT, NE)
        pick1 = route(NT, NE)
        pick2 = route(NT, NE)
        pick = route(NT, NE)
        top1 = route(NT)
        top2 = route(NT)
        hid_flat, sig_flat = hid[:], sig_exp[:]
        counts = carve(hid_flat, (4 * NE,), rank_at)
        first_row = carve(hid_flat, (NE,), rank_at)
        more = carve(hid_flat, (NE,), rank_at)
        more_at = carve(hid_flat, (NE,), rank_at)
        jump = carve(sig_flat, (NE,), place_at)
        place = carve(sig_flat, (NT, NE), place_at)
        picked = carve(sig_flat, (NT, NE), place_at)
        sums = sb("sums", [P, 4, NT])
        ov = (ple_sig[0:1, 0:NOV * NE], ple_tmp[0:1, 0:NOV * NE], route(NOV * NE)[0:1])
        sums_ov = sb("sums_ov", [1, NOV])
        in_use = sb("in_use", [1, NOV])
        t_used = [0]
        tb = carve(m_flat, (2, 2, JC, T), t_used)
        ssmT = carve(m_flat, (NCH, T), [0])
        sq = carve(m_flat, (NCH, T), [NCH * T])
        tp1 = carve(hT[:].rearrange("p k t -> p (k t)"), (2, JC, P), [0])
        tp2 = carve(hT[:].rearrange("p k t -> p (k t)"), (2, JC, P), [2 * JC * P])
        tail = [10 * D]
        v_rows = carve(e_flat, (P,), tail)[0:nvec, :]
        pr = carve(e_flat, (18, P), tail)[0:NJ]
        p_rows = carve(e_flat, (NT, PLC * P), tail)
        zeros_x = hT[:].rearrange("p k t -> p (k t)")[0:B, 2048:2048 + D]
        assert used[0] <= 10 * D, used

        x_landed = sem("x_landed")
        small_landed = sem("small_landed")
        vec_landed = sem("vec_landed")
        p_landed = sem("p_landed")
        router_landed = sem("router_landed")
        pool_own = sem("pool_own")
        dve_own = sem("dve_own")
        act_own = sem("act_own")
        ident_ready = sem("ident_ready")
        masks_ready = sem("masks_ready")
        pad_stored = sem("pad_stored")
        var_ready = sem("var_ready")
        rstd_ready = sem("rstd_ready")
        xn_ready = sem("xn_ready")
        vecT_ready = sem("vecT_ready")
        vecT_copied = sem("vecT_copied")
        xt_ready = sem("xt_ready")
        xt_even = sem("xt_even")
        xt_odd = sem("xt_odd")
        pt_ready = sem("pt_ready")
        pt_copied = sem("pt_copied")
        pr_act_in = sem("pr_act_in")
        pr_act_out = sem("pr_act_out")
        pr_ready = sem("pr_ready")
        parT_ready = sem("parT_ready")
        par_copied = sem("par_copied")
        coef_ready = sem("coef_ready")
        w_landed = [sem(f"w_landed{s}") for s in range(4)]
        dense_done = sem("dense_done")
        bc_landed = sem("bc_landed")
        bc_ready = sem("bc_ready")
        bcT_ready = sem("bcT_ready")
        bcT_copied = sem("bcT_copied")
        table_ready = sem("table_ready")
        ck_landed = sem("ck_landed")
        cv_landed = sem("cv_landed")
        proj_copied = sem("proj_copied")
        ckT_ready = sem("ckT_ready")
        ckT_copied = sem("ckT_copied")
        du_ready = sem("du_ready")
        bu_ready = sem("bu_ready")
        bu_used = sem("bu_used")
        h_ready = sem("h_ready")
        y_part = sem("y_part")
        y_read = sem("y_read")
        last_ready = sem("last_ready")
        gelu_in = sem("gelu_in")
        gelu_sig = sem("gelu_sig")
        z_done = sem("z_done")
        z_ready = sem("z_ready")
        zm_ready = sem("zm_ready")
        sig_ready = sem("sig_ready")
        wgt_ready = sem("wgt_ready")
        wT_ready = sem("wT_ready")
        wT_copied = sem("wT_copied")
        kn_ready = sem("kn_ready")
        kn_copied = sem("kn_copied")
        vn_ready = sem("vn_ready")
        vn_copied = sem("vn_copied")
        k_stored = sem("k_stored")
        v_stored = sem("v_stored")
        a_ready = sem("a_ready")
        a_copied = sem("a_copied")
        lastT_ready = sem("lastT_ready")
        last_copied = sem("last_copied")
        last_stored = sem("last_stored")
        asq_ready = sem("asq_ready")
        ass_ready = sem("ass_ready")
        glu_sig = sem("glu_sig")
        s_ready = sem("s_ready")
        ssq_ready = sem("ssq_ready")
        sss_ready = sem("sss_ready")
        ms_ready = sem("ms_ready")
        rms_root = sem("rms_root")
        rms_ready = sem("rms_ready")
        merged_a = sem("merged_a")
        merged_s = sem("merged_s")
        res_ready = sem("res_ready")
        nat_ready = sem("nat_ready")
        var1_ready = sem("var1_ready")
        rstd1_ready = sem("rstd1_ready")
        nm1_ready = sem("nm1_ready")
        xh_ready = sem("xh_ready")
        gb1_landed = sem("gb1_landed")
        hg_ready = sem("hg_ready")
        h_rows_ready = sem("h_rows_ready")
        hT_ready = sem("hT_ready")
        hT_copied = sem("hT_copied")
        logits_ready = sem("logits_ready")
        exp_in = sem("exp_in")
        exp_out = sem("exp_out")
        pick_ready = sem("pick_ready")
        rank_ready = sem("rank_ready")
        idx_ready = sem("idx_ready")
        tab_ready = sem("tab_ready")
        rows_sorted = sem("rows_sorted")
        ew_landed = [sem(f"ew_landed{s}") for s in range(NEW)]
        ew_used = sem("ew_used")
        xe_landed = sem("xe_landed")
        xeT_ready = sem("xeT_ready")
        xeT_act = sem("xeT_act")
        xeT_dve = sem("xeT_dve")
        gsig_ready = sem("gsig_ready")
        gmul_ready = sem("gmul_ready")
        hid_ready = sem("hid_ready")
        hidT_ready = sem("hidT_ready")
        hidT_copied = sem("hidT_copied")
        ye_act = sem("ye_act")
        ye_dve = sem("ye_dve")
        ye_stored = sem("ye_stored")
        plg_sig = sem("plg_sig")
        ple_mul = sem("ple_mul")
        ple_done = sem("ple_done")
        all_stored = sem("all_stored")
        gb2_landed = sem("gb2_landed")
        y_gathered = [sem(f"y_gathered{t}") for t in range(NT)]
        fin_nat = sem("fin_nat")
        fin_var = sem("fin_var")
        fin_sum = sem("fin_sum")
        fin_rstd = sem("fin_rstd")
        fin_nm = sem("fin_nm")
        fin_xh = sem("fin_xh")
        fin_g = sem("fin_g")
        fin_b = sem("fin_b")
        y_stored = sem("y_stored")

        block = ctx.enter_context(nc.Block())

        N_GLU = 4 * NCH
        N_OUT = N_GLU + NCH
        N_PLE = N_OUT + KC
        LAST_C = NCH

        def further_blocks(eng, body):
            count = eng.value_load(tab[0:1, NTAB + NOV:NTAB + NOV + 1], min_val=0, max_val=NOV)
            with eng.Fori(0, NOV) as i:
                with eng.If(count > i):
                    body(i)
            return count

        @block.sync
        def _(sp):
            for t, (_, m) in enumerate(TT):
                sp.dma_start(rows[0:m, t, :], x_src[t]).then_inc(x_landed, 16)
            for name, src, n in vec_list:
                a = vec_at[name]
                sp.dma_start(v_rows[a:a + n, :], src.rearrange("(k p) -> k p", p=P)).then_inc(vec_landed, 16)
            for f, src in enumerate(rows_v):
                sp.dma_start(pr[:, f, :], src).then_inc(small_landed, 16)
            with nc.allow_non_contiguous_dma(reason="64 values"):
                sp.dma_start(pr[:, 4, 0:2], step_v).then_inc(small_landed, 16)

            def settled():
                sp.wait_ge(x_landed, 16 * NT)

            def w_load(slot, wait, src, width=P):
                if wait is not None:
                    sp.wait_ge(dense_done, wait)
                    settled()
                sp.dma_start(w_ring[:, slot, 0:src.shape[1] * width].rearrange("p (k n) -> p k n", n=width),
                             src).then_inc(w_landed[slot], 16)

            def chunk(c, first):
                if not first:
                    sp.wait_ge(bc_ready, c)
                    settled()
                for r in range(2):
                    sp.dma_start(bf[:, r], b_v[r][:, c]).then_inc(bc_landed, 16)
                    sp.dma_start(cf[:, r], c_v[r][:, c]).then_inc(bc_landed, 16)
                for s, part in enumerate((3, 0, 1, 2)):
                    if s == 1:
                        if not first:
                            settled()
                            sp.wait_ge(ckT_ready, c)
                        sp.dma_start(ck, ck_v[:, :, c, :]).then_inc(ck_landed, 16)
                    w_load(s, None if first else c * 4 + (s - 3),
                           w_in_v[:, :, ds(part * W + c * P, P)])

            chunk(0, True)
            for t, (_, m) in enumerate(TT):
                sp.dma_start(p_rows[0:m, t, :], p_src[t]).then_inc(p_landed, 16)
            sp.dma_start(w_router[:, :, 0:NGRP], w_router_group[0].rearrange("(k p) n -> p k n", p=P)).then_inc(router_landed, 16)
            sp.dma_start(w_router[:, :, NGRP:RW], w_router_expert[0].rearrange("(k p) n -> p k n", p=P)).then_inc(router_landed, 16)
            sp.dma_start(b_router[:, 0:NGRP], b_router_group[0].partition_broadcast(P)).then_inc(router_landed, 16)
            sp.dma_start(b_router[:, NGRP:RW], b_router_expert[0].partition_broadcast(P)).then_inc(router_landed, 16)
            with sp.Fori(1, NCH) as c:
                chunk(c, False)
            for s in range(4):
                w_load(s, N_GLU + s - 3, w_glu_v[:, :, 2 * s * P:2 * (s + 1) * P], 2 * P)
            for s in range(4):
                w_load(s, N_GLU + 2 * s + 2, w_out_v[:, :, s * P:(s + 1) * P])

            def expert_piece(b, e, s, first):
                if not first:
                    sp.wait_ge(ew_used, b * NEW + (s + 1 - NEW))
                    settled()
                if s < 8:
                    src = (wg_v, wu_v)[s % 2][:, ds(e, 1), 4 * (s // 2):4 * (s // 2) + 4, :]
                    dst = e_ring[:, s, :].rearrange("p (a k f) -> p a k f", a=1, k=4)
                else:
                    src = wd_v[:, ds(e, 1), s - 8, :]
                    dst = e_ring[:, s:s + 1, :]
                sp.dma_start(dst, src).then_inc(ew_landed[s], 16)

            def expert_load(b, e):
                for s in range(NEW):
                    expert_piece(b, e, s, False)

            sp.wait_ge(merged_s, NCH)
            sp.wait_ge(last_stored, 64)
            sp.wait_ge(pt_copied, PLC)
            for m in range(4, KC):
                w_load(m % 4, N_OUT + m - 3, w_out_v[:, :, m * P:(m + 1) * P])
                expert_piece(0, 0, m - 4, True)
            sp.wait_ge(dense_done, N_PLE)
            sp.dma_start(w_ring[:, 2, :], ln1_g[0].partition_broadcast(P)).then_inc(gb1_landed, 16)
            sp.dma_start(w_ring[:, 3, :], ln1_b[0].partition_broadcast(P)).then_inc(gb1_landed, 16)

            def ple_load(i, wait):
                sp.wait_ge(dense_done, wait)
                settled()
                sp.dma_start(w_ring[:, 0, :].rearrange("p (k n) -> p k n", n=P), w_plg_v[:, :, ds(i * P, P)]).then_inc(w_landed[0], 16)
                sp.dma_start(w_ring[:, 1, 0:PLC * P].rearrange("p (k n) -> p k n", n=P), w_plp_v[:, :, ds(i * P, P)]).then_inc(w_landed[1], 16)

            ple_load(0, N_PLE)
            expert_load(1, 1)
            sp.wait_ge(h_rows_ready, NT)
            sp.dma_start(w_ring[:, 2, :], ln2_g[0].partition_broadcast(P)).then_inc(gb2_landed, 16)
            sp.dma_start(w_ring[:, 3, :], ln2_b[0].partition_broadcast(P)).then_inc(gb2_landed, 16)
            with sp.Fori(1, NE // 2) as i:
                ple_load(i, i * 2 + N_PLE)
                expert_load(i * 2, i * 2)
                expert_load(i * 2 + 1, i * 2 + 1)
            sp.wait_ge(tab_ready, 1)

            def further(i):
                e = sp.value_load(tab[0:1, ds(i + NTAB, 1)], min_val=0, max_val=NE - 1)
                expert_load(i + NE, e)

            further_blocks(sp, further)
            for t, (_, m) in enumerate(TT):
                sp.wait_ge(fin_b, t + 1)
                sp.dma_start(y_dst[t], e_ring[0:m, t, :]).then_inc(y_stored, 16)
            sp.wait_ge(y_stored, 16 * NT)

        @block.gpsimd
        def _(pool):
            own = OwnOrder(pool, pool_own)
            own(pool.memset(ident[:], 0.0))
            own(pool.memset(ones[:], 1.0))
            own(pool.memset(mask, 0.0))
            own(pool.memset(mask_s, 0.0))
            own(pool.memset(zeros_x, 0.0))
            own(pool.memset(neg_half[:], -0.5))
            own.wait()
            pool.affine_select(out=ident[:], in_=ident[:], compare_op=ALU.not_equal, fill=1.0, base=0,
                               pattern=[[-1, P]], channel_multiplier=1).then_inc(ident_ready, 1)
            pool.dma_start(xs_dram[2 * T:XROWS, :], zeros_x).then_inc(pad_stored, 16)
            for i in range(NOV):
                pool.dma_start(ys_dram[(NE + i) * B:(NE + i + 1) * B, :], zeros_x).then_inc(pad_stored, 16)
            own(pool.affine_select(out=upper[:], in_=ones[:], compare_op=ALU.is_gt, fill=0.0, base=0,
                                   pattern=[[1, P]], channel_multiplier=-1))
            for view, m in ((mask[:, 0:P], P), (mask[:, P + P:P + 2 * P], P), (mask_s[0:TS, PAST:PAST + TS], TS)):
                own(pool.affine_select(out=view, in_=view, compare_op=ALU.is_gt, fill=NEG, base=0,
                                       pattern=[[-1, m]], channel_multiplier=1))
            own(pool.affine_select(out=par_b[:, 0:1], in_=ones[:, 0:1], compare_op=ALU.is_ge, fill=0.0, base=NS - 1,
                                   pattern=[[0, 1]], channel_multiplier=-1))
            own(pool.affine_select(out=par_b[:, 1:2], in_=ones[:, 0:1], compare_op=ALU.is_ge, fill=0.0, base=-NS,
                                   pattern=[[0, 1]], channel_multiplier=1))
            own(pool.affine_select(out=g8[:], in_=ones[:, 0:P // GC], compare_op=ALU.is_ge, fill=0.0, base=0,
                                   pattern=[[-GC, P // GC]], channel_multiplier=1))
            own.wait()
            own(pool.affine_select(out=g8[:], in_=g8[:], compare_op=ALU.is_ge, fill=0.0, base=GC - 1,
                                   pattern=[[GC, P // GC]], channel_multiplier=-1))
            own.wait()
            g8v = g8[:].rearrange("p (i a) -> p a i", a=2)
            pool.tensor_tensor(tmp1[:, 0, 0:4].rearrange("p (a i) -> p a i", a=2), g8v[:, :, 0:2], g8v[:, :, 2:4], ALU.add).then_inc(pool_own, 1)
            own.n += 1
            own.wait()
            t1v = tmp1[:, 0, 0:4].rearrange("p (a i) -> p a i", a=2)
            own(pool.tensor_tensor(par_cg[:], t1v[:, :, 0], t1v[:, :, 1], ALU.add))
            own.wait()
            pool.iota(io[:], [[1, NE]], base=0, channel_multiplier=0,
                      allow_small_or_imprecise_dtypes=True).then_inc(masks_ready, 1)
            pool.wait_ge(var_ready, NT)
            pool.tensor_tensor(rstd[:], var_eps[:], neg_half[:, 0:1].to_broadcast([P, NT]), ALU.pow).then_inc(rstd_ready, 1)

            pool.wait_ge(coef_ready, 1)
            pool.wait_ge(xt_ready, KC)
            pool.wait_ge(pad_stored, 16 * (NOV + 1))

            def chunk(c, cb, first, early_chunk=False):
                pool.wait_ge(bc_landed, c * 64 + 64)
                if not first:
                    pool.wait_ge(bcT_ready, c)
                pool.wait_ge(coef_ready, 1)
                shp = [P, JC, 2, GC]
                bre, bim = (bf[:, r].unsqueeze(2).to_broadcast(shp) for r in range(2))
                cre, cim = (coef[:, r, ds(c * JC, JC), :].unsqueeze(3).to_broadcast(shp) for r in range(2))
                own(pool.tensor_tensor(bt[:, 0], bre, cre, ALU.mult))
                own(pool.tensor_tensor(bt[:, 1], bim, cim, ALU.mult))
                own(pool.tensor_tensor(bt[:, 2], bre, cim, ALU.mult))
                own(pool.tensor_tensor(bt[:, 3], bim, cre, ALU.mult))
                for a in range(2):
                    own(pool.tensor_scalar(cn[:, 0, a, :], cf[:, 0, :], par_cg[:, a:a + 1], 1.0, ALU.mult, ALU.mult))
                    own(pool.tensor_scalar(cn[:, 1, a, :], cf[:, 1, :], par_cg[:, a:a + 1], -1.0, ALU.mult, ALU.mult))
                own.wait()
                own(pool.tensor_tensor(bn[:, 0], bt[:, 0], bt[:, 1], ALU.subtract))
                own.wait()
                pool.tensor_tensor(bn[:, 1], bt[:, 2], bt[:, 3], ALU.add).then_inc(bc_ready, 1)
                if not early_chunk:
                    pool.wait_ge(last_ready, (c - 1) * JC)
                    pool.wait_ge(coef_ready, 1)
                w = tb[:, cb]
                own(pool.tensor_tensor(w[:, :, :, 0], par[:, 1:3, ds(c * JC, JC)],
                                       ones[:, 0:2 * JC].rearrange("p (r j) -> p r j", r=2), ALU.mult))
                own.wait()
                k = 1
                while k < TP:
                    s4 = [P, 2, JC, k]
                    own(pool.tensor_tensor(tp1[:, :, :, 0:k], w[:, :, :, 0:k],
                                           w[:, 0:1, :, k - 1:k].to_broadcast(s4), ALU.mult))
                    own(pool.tensor_tensor(tp2[:, :, :, 0:k], w[:, :, :, 0:k],
                                           w[:, 1:2, :, k - 1:k].to_broadcast(s4), ALU.mult))
                    own.wait()
                    own(pool.tensor_tensor(w[:, 0, :, k:2 * k], tp1[:, 0, :, 0:k], tp2[:, 1, :, 0:k], ALU.subtract))
                    own(pool.tensor_tensor(w[:, 1, :, k:2 * k], tp1[:, 1, :, 0:k], tp2[:, 0, :, 0:k], ALU.add))
                    own.wait()
                    k *= 2
                pool.tensor_tensor(w[:, :, :, TP:T], w[:, :, :, 0:TS],
                                   ones[:, 0:1].unsqueeze(1).unsqueeze(1).to_broadcast([P, 2, JC, TS]), ALU.mult).then_inc(table_ready, 1)

            chunk(0, 0, True, True)
            chunk(1, 1, False, True)
            base = own.base + own.n
            with pool.Fori(1, NCH // 2) as i:
                own.enter((i - 1) * POOL_PER_PAIR + base)
                chunk(i * 2, 0, False)
                chunk(i * 2 + 1, 1, False)
                assert own.n == POOL_PER_PAIR, own.n
            own.enter(base + (NCH // 2 - 1) * POOL_PER_PAIR)
            for t, (_, m) in enumerate(TT):
                pool.wait_ge(var1_ready, t + 1)
                pool.tensor_tensor(rstd[0:m, t:t + 1], var_eps[0:m, t:t + 1], neg_half[0:m, :], ALU.pow).then_inc(rstd1_ready, 1)
            for t, (_, m) in enumerate(TT):
                pool.wait_ge(hg_ready, t + 1)
                pool.tensor_tensor(rows[0:m, t, :], rows[0:m, t, :], w_ring[0:m, 3, :], ALU.add).then_inc(h_rows_ready, 1)
            pool.wait_ge(idx_ready, 1)
            pool.wait_ge(h_rows_ready, NT)
            for k in range(2):
                for t, (_, m) in enumerate(TT):
                    pool.indirect_dma_start(xs_dram[:, :], bass.IndirectOffsetOnAxis(ap=idx[0:m, k, t:t + 1], axis=0),
                                            rows[0:m, t, :], None).then_inc(rows_sorted, 16)
            pool.wait_ge(all_stored, 1)
            for t, (_, m) in enumerate(TT):
                for k in range(2):
                    pool.indirect_dma_start(e_ring[0:m, k * NT + t, :], None, ys_dram[:, :],
                                            bass.IndirectOffsetOnAxis(ap=idx[0:m, 2 + k, t:t + 1], axis=0)).then_inc(y_gathered[t], 16)
            for t, (_, m) in enumerate(TT):
                pool.wait_ge(fin_var, t + 1)
                pool.tensor_tensor(rstd[0:m, t:t + 1], var_eps[0:m, t:t + 1], neg_half[0:m, :], ALU.pow).then_inc(fin_rstd, 1)
            for t, (_, m) in enumerate(TT):
                pool.wait_ge(fin_g, t + 1)
                pool.tensor_tensor(e_ring[0:m, t, :], e_ring[0:m, t, :], w_ring[0:m, 3, :], ALU.add).then_inc(fin_b, 1)

        @block.scalar
        def _(act):
            def copy(out, in_):
                return act.activation(out, in_, ACT.Copy)

            act.wait_ge(small_landed, 80)
            act.activation(pr[:, 4, 2:4], pr[:, 4, 0:2], ACT.Exp).then_inc(pr_act_out, 1)
            act.wait_ge(pr_act_in, 1)
            act.activation(pr[:, 8, :], pr[:, 5, :], ACT.Exp).then_inc(pr_act_out, 1)
            act.activation(pr[:, 9:11, :], pr[:, 11:13, :], ACT.Sin).then_inc(pr_act_out, 1)
            act.wait_ge(vecT_ready, 1)
            copy(vecT[:], bank[:, 7, 0:nvec]).then_inc(vecT_copied, 1)
            act.wait_ge(vecT_copied, 1)
            for k in range(0, KC, 2):
                act.wait_ge(xt_ready, k + 1)
                a, b = vec_at["ln_in_g"] + k, vec_at["ln_in_b"] + k
                act.activation(xT[:, k, :], bank[:, k % 4, 0:T], ACT.Identity, scale=vecT[:, a:a + 1],
                               bias=vecT[:, b:b + 1]).then_inc(xt_even, 1)
            act.wait_ge(parT_ready, 1)
            copy(par[:].rearrange("p f j -> p (f j)"), bank[:, 5, 0:7 * NJ]).then_inc(par_copied, 1)
            for k in range(PLC):
                act.wait_ge(pt_ready, k + 1)
                copy(pT[:, k, :], bank[:, 4 if k else 6, 0:T]).then_inc(pt_copied, 1)

            def chunk(c, cur, prev, first):
                if cur:
                    act.wait_ge(dense_done, c * 4 + 1)
                    if prev:
                        act.wait_ge(du_ready, c)
                    copy(uT, bank[:, 0, 0:T]).then_inc(proj_copied, 1)
                    act.wait_ge(bcT_ready, c + 1)
                    copy(bcT.rearrange("p f n -> p (f n)"), bank[:, 7, 0:4 * P]).then_inc(bcT_copied, 1)
                if prev:
                    act.wait_ge(zm_ready, c)
                    if not first:
                        act.wait_ge(wgt_ready, c - 1)
                    act.activation(sig[:, 0:Z2], zm[:, 0:Z2], ACT.Sigmoid)
                    act.activation(sig[0:TS, Z2:ZW], zm[0:TS, Z2:ZW], ACT.Sigmoid)
                    act.activation(keep[:, 0:Z2], zm[:, 0:Z2], ACT.Sigmoid, scale=-1.0)
                    act.activation(keep[0:TS, Z2:ZW], zm[0:TS, Z2:ZW], ACT.Sigmoid, scale=-1.0).then_inc(sig_ready, 1)
                    act.wait_ge(kn_ready, c)
                    if not first:
                        act.wait_ge(k_stored, (c - 1) * 32)
                    copy(k_nat[:, 0:2, :], bank[:, 7, 0:2 * P].rearrange("p (t n) -> p t n", t=2)).then_inc(kn_copied, 1)
                    copy(k_nat[0:TS, 2, :], bank[0:TS, 7, 2 * P:3 * P]).then_inc(kn_copied, 1)
                    act.wait_ge(kn_copied, c * 2)
                    act.dma_start(kp_v[:, :, c - 1, :], k_nat[:, 0:2, :]).then_inc(k_stored, 16)
                    act.dma_start(k_sample[0, 0, :, c - 1, :], k_nat[0:TS, 2, :]).then_inc(k_stored, 16)
                    act.wait_ge(gelu_in, c)
                    if not first:
                        act.wait_ge(z_done, c - 1)
                    act.activation(ysig, y2, ACT.Sigmoid, scale=2.0 * math.sqrt(2.0 / math.pi) * 0.044715).then_inc(gelu_sig, 1)
                if cur:
                    act.wait_ge(dense_done, c * 4 + 2)
                    copy(qT, bank[:, 1, 0:T]).then_inc(proj_copied, 1)
                    act.wait_ge(ckT_ready, c + 1)
                    copy(ckT, bank[:, 7, 0:PAST]).then_inc(ckT_copied, 1)
                    act.wait_ge(dense_done, c * 4 + 3)
                    copy(kT, bank[:, 0, 0:T]).then_inc(proj_copied, 1)
                if prev:
                    act.wait_ge(vn_ready, c)
                    if not first:
                        act.wait_ge(v_stored, (c - 1) * 32)
                    copy(v_nat[:, 0:2, :], bank[:, 7, 0:2 * P].rearrange("p (t n) -> p t n", t=2)).then_inc(vn_copied, 1)
                    copy(v_nat[0:TS, 2, :], bank[0:TS, 7, 2 * P:3 * P]).then_inc(vn_copied, 1)
                    act.wait_ge(wT_ready, c)
                    copy(wT[:, 0:448], bank[:, 5, 0:448]).then_inc(wT_copied, 1)
                    copy(wT[0:TS, 448:480], bank[0:TS, 5, 448:480]).then_inc(wT_copied, 1)
                    act.wait_ge(vn_copied, c * 2)
                    act.dma_start(vp_v[:, :, c - 1, :], v_nat[:, 0:2, :]).then_inc(v_stored, 16)
                    act.dma_start(v_sample[0, 0, :, c - 1, :], v_nat[0:TS, 2, :]).then_inc(v_stored, 16)
                if cur:
                    act.wait_ge(dense_done, c * 4 + 4)
                    copy(vT, bank[:, 1, 0:T]).then_inc(proj_copied, 1)
                if prev:
                    act.wait_ge(a_ready, c)
                    copy(attnT[:, ds(c - 1, 1), :].rearrange("p a t -> p (a t)"), bank[:, 6, 0:T]).then_inc(a_copied, 1)
                if cur:
                    act.dma_start(cv, cv_v[:, :, c, :]).then_inc(cv_landed, 16)

            chunk(0, True, False, True)
            chunk(1, True, True, True)
            with act.Fori(2, NCH) as c:
                chunk(c, True, True, False)
            chunk(LAST_C, False, True, False)

            act.wait_ge(a_copied, NCH)
            act.wait_ge(last_ready, NJ)
            act.activation(sq, attnT, ACT.Square).then_inc(asq_ready, 1)
            act.wait_ge(lastT_ready, 1)
            copy(last_rows[0:NJ], bank[0:NJ, 6, 0:4 * P].rearrange("p (f n) -> p f n", f=4)).then_inc(last_copied, 1)
            act.wait_ge(last_copied, 1)
            for f in range(4):
                act.dma_start(last_v[f], last_rows[0:NJ, f, :]).then_inc(last_stored, 16)
            act.wait_ge(ms_ready, 1)
            act.activation(rms_a, rms_a, ACT.Sqrt).then_inc(rms_root, 1)
            for m in range(NCH + 1):
                if m < NCH:
                    act.wait_ge(dense_done, N_GLU + m + 1)
                    if m >= 2:
                        act.wait_ge(s_ready, m - 1)
                    a = vec_at["b_glu"] + m
                    act.activation(sg[:, m % 2], bank[:, m % 2, 0:T], ACT.Sigmoid, bias=vecT[:, a:a + 1]).then_inc(glu_sig, 1)
                if m:
                    act.wait_ge(s_ready, m)
                    act.activation(sq[:, m - 1], ssmT[:, m - 1], ACT.Square).then_inc(ssq_ready, 1)
            act.wait_ge(ms_ready, 2)
            act.activation(rms_s, rms_s, ACT.Sqrt).then_inc(rms_root, 1)
            for t, (_, m) in enumerate(TT):
                act.wait_ge(nm1_ready, t + 1)
                b0 = 4 * (t % 2)
                act.activation(rows[0:m, t, :], bank[0:m, b0:b0 + 4, :].rearrange("p b n -> p (b n)"), ACT.Identity,
                               scale=rstd[0:m, t:t + 1], bias=neg_mean[0:m, t:t + 1]).then_inc(xh_ready, 1)
            for t, (t0, m) in enumerate(TT):
                for q in range(4):
                    act.wait_ge(hT_ready, 4 * t + q + 1)
                    copy(hT[:, 4 * q:4 * q + 4, t0:t0 + m], bank[:, (4, 0, 4)[t] + q, 0:4 * m].rearrange("p (k n) -> p k n", k=4)).then_inc(hT_copied, 1)
            act.wait_ge(exp_in, 1)
            act.activation(e5, d5, ACT.Exp).then_inc(exp_out, 1)

            def x_load(b):
                row = act.value_load(tab[0:1, ds(b, 1)], min_val=0, max_val=2 * T)
                for h in range(2):
                    act.dma_start(x_exp[h * B:(h + 1) * B, :], xs_dram[ds(row, B), h * DH2:(h + 1) * DH2]).then_inc(xe_landed, 16)

            def x_copy(b):
                act.wait_ge(xeT_ready, b + 1)
                copy(xT_exp[:, 0:4].rearrange("p k h n -> p (k h n)"), bank[:, 1, :]).then_inc(xeT_act, 1)

            def expert(b, first, middle=None):
                act.wait_ge(ew_used, b * NEW + 8)
                act.activation(sig_exp[:], bank[:, 0, 0:FH], ACT.Sigmoid).then_inc(gsig_ready, 1)
                x_copy(b + 1)
                x_load(b + 2)
                if middle is not None:
                    middle()
                act.wait_ge(ew_used, b * NEW + NEW)
                if not first:
                    act.wait_ge(ye_stored, b * 32)
                copy(y_exp[:, 0:512], bank[:, 3, :]).then_inc(ye_act, 1)
                act.wait_ge(ye_act, b + 1)
                act.wait_ge(ye_dve, b + 1)
                for h in range(2):
                    act.dma_start(ys_dram[ds(b * B, B), h * DH2:(h + 1) * DH2], y_exp[h * B:(h + 1) * B, :]).then_inc(ye_stored, 16)

            def pair(i, first):
                def gate_sig():
                    act.wait_ge(dense_done, i * 2 + (N_PLE + 1))
                    if not first:
                        act.wait_ge(ple_mul, i)
                    act.activation(ple_sig[:], bank[:, 7, 0:T], ACT.Sigmoid).then_inc(plg_sig, 1)
                expert(i * 2, first, gate_sig)
                expert(i * 2 + 1, False)

            act.wait_ge(tab_ready, 1)
            act.wait_ge(rows_sorted, 16 * 2 * NT)
            x_load(0)
            x_copy(0)
            x_load(1)
            pair(0, True)
            with act.Fori(1, NE // 2) as i:
                pair(i, False)
            count = further_blocks(act, lambda i: expert(i + NE, False))
            act.wait_ge(ye_stored, count * 32 + NE * 32)
            act.wait_ge(xe_landed, count * 32 + (NE + 2) * 32)
            copy(flag[0:1, 0:1], zero_col[0:1, 0:1]).then_inc(all_stored, 1)
            for t, (_, m) in enumerate(TT):
                act.wait_ge(fin_nm, t + 1)
                act.activation(e_ring[0:m, t, :], e_ring[0:m, t, :], ACT.Identity,
                               scale=rstd[0:m, t:t + 1], bias=neg_mean[0:m, t:t + 1]).then_inc(fin_xh, 1)

        @block.tensor
        def _(pe):
            def dense(out, weights, moving, n):
                for k in range(n):
                    last_mm = pe.matmul(out, weights(k), moving[:, k, :], start=(k == 0), stop=(k == n - 1))
                return last_mm

            pe.wait_ge(ident_ready, 1)
            pe.wait_ge(vec_landed, 16 * len(vec_list))
            pe.transpose(bank[:, 7, 0:nvec], v_rows, ident[0:nvec, 0:nvec]).then_inc(vecT_ready, 1)
            pe.wait_ge(xn_ready, NT)
            for k in range(KC):
                if k >= 4:
                    pe.wait_ge(xt_odd if k % 2 else xt_even, (k - 4) // 2 + 1)
                for t, (t0, m) in enumerate(TT):
                    mm = pe.transpose(bank[:, k % 4, t0:t0 + m], rows[0:m, t, k * P:(k + 1) * P], ident[0:m, 0:m])
                mm.then_inc(xt_ready, 1)
            pe.wait_ge(pr_ready, 1)
            for i, f in enumerate((8, 9, 10, 16, 17, 2, 3)):
                mm = pe.transpose(bank[:, 5, i * NJ:(i + 1) * NJ], pr[:, f, :], ident[0:NJ, 0:NJ])
            mm.then_inc(parT_ready, 1)
            pe.wait_ge(p_landed, 48)
            for k in range(PLC):
                for t, (t0, m) in enumerate(TT):
                    mm = pe.transpose(bank[:, 4 if k else 6, t0:t0 + m], p_rows[0:m, t, k * P:(k + 1) * P], ident[0:m, 0:m])
                mm.then_inc(pt_ready, 1)
            pe.wait_ge(xt_even, KC // 2)
            pe.wait_ge(xt_odd, KC // 2)
            pe.wait_ge(par_copied, 1)
            pe.wait_ge(pt_copied, PLC)

            def proj(c, s, first):
                pe.wait_ge(w_landed[s], c * 16 + 16)
                if not (first and s < 2):
                    pe.wait_ge(proj_copied, c * 4 + s - 1)
                w = w_ring[:, s, :].rearrange("p (k n) -> p k n", n=P)
                dense(bank[:, s % 2, 0:T], lambda k: w[:, k, :], xT, KC).then_inc(dense_done, 1)

            def bu(c, i, first):
                if not (first and i == 0):
                    pe.wait_ge(bu_used, c * JC + i)
                for r in range(2):
                    mm = pe.matmul(bank[:, 2 + r, 0:T], bcT[32 * i:32 * i + 32, r, :], uT[32 * i:32 * i + 32, :], start=True, stop=True)
                mm.then_inc(bu_ready, 1)

            def y_out(c, i):
                pe.wait_ge(h_ready, c * JC + i + 1)
                for r in range(2):
                    mm = pe.matmul(bank[32 * i:32 * i + 32, 4, 0:T], bcT[:, 2 + r, 32 * i:32 * i + 32], h_ssm[:, i % 2, r, :],
                                   start=(r == 0), stop=(r == 1))
                mm.then_inc(y_part, 1)

            def chunk(c, cur, prev, first):
                if cur:
                    proj(c, 0, not prev)
                if prev:
                    y_out(c - 1, 3)
                if cur:
                    pe.wait_ge(bc_ready, c + 1)
                    if prev and not first:
                        pe.wait_ge(vn_copied, (c - 1) * 2)
                    if prev:
                        pe.wait_ge(ckT_copied, c)
                    for r in range(2):
                        pe.transpose(bank[:, 7, r * P:(r + 1) * P], bn[:, r].rearrange("p j a n -> p (j a n)"), ident[:])
                    for r in range(2):
                        mm = pe.transpose(bank[:, 7, (2 + r) * P:(3 + r) * P], cn[:, r].rearrange("p a n -> p (a n)"), ident[:])
                    mm.then_inc(bcT_ready, 1)
                if prev:
                    pe.wait_ge(proj_copied, c * 4)
                    if not first:
                        pe.wait_ge(wT_copied, (c - 1) * 2)
                        pe.wait_ge(a_copied, c - 1)
                    pe.wait_ge(ckT_copied, c)
                    pe.matmul(bank[:, 5, 0:Z1], qT[:, 0:P], kT[:, 0:P], start=True, stop=True)
                    pe.matmul(bank[:, 5, Z1:Z2], qT[:, P:TP], kT[:, 0:TP], start=True, stop=True)
                    pe.matmul(bank[0:TS, 6, 0:PAST], qT[:, TP:T], ckT, start=True, stop=True)
                    pe.matmul(bank[0:TS, 6, PAST:PAST + TS], qT[:, TP:T], kT[:, TP:T], start=True, stop=True).then_inc(z_ready, 1)
                if cur:
                    pe.wait_ge(proj_copied, c * 4 + 1)
                    pe.wait_ge(bcT_copied, c + 1)
                    bu(c, 0, not prev)
                if prev:
                    if cur is False:
                        pe.wait_ge(ckT_copied, c)
                    for t, (t0, m) in enumerate(TT):
                        mm = pe.transpose(bank[0:m, 7, t * P:(t + 1) * P], kT[:, t0:t0 + m], ident[:])
                    mm.then_inc(kn_ready, 1)
                if cur:
                    proj(c, 1, not prev)
                    pe.wait_ge(ck_landed, c * 16 + 16)
                    if prev:
                        pe.wait_ge(kn_copied, c * 2)
                    for t in range(2):
                        mm = pe.transpose(bank[:, 7, t * P:(t + 1) * P], ck[:, t, :], ident[:])
                    mm.then_inc(ckT_ready, 1)
                    bu(c, 1, False)
                    if prev:
                        pe.wait_ge(y_read, c)
                    y_out(c, 0)
                    proj(c, 2, not prev)
                if prev:
                    pe.wait_ge(ckT_copied, c + 1) if cur else pe.wait_ge(kn_copied, c * 2)
                    for t, (t0, m) in enumerate(TT):
                        mm = pe.transpose(bank[0:m, 7, t * P:(t + 1) * P], vT[:, t0:t0 + m], ident[:])
                    mm.then_inc(vn_ready, 1)
                if cur:
                    bu(c, 2, False)
                    y_out(c, 1)
                if prev:
                    pe.wait_ge(wgt_ready, c)
                    pe.transpose(bank[:, 5, 0:P], wgt[:, 0:P], ident[:])
                    pe.transpose(bank[:, 5, P:2 * P], wgt[:, Z1:Z1 + P], ident[:])
                    pe.transpose(bank[:, 5, 2 * P:3 * P], wgt[:, Z1 + P:Z2], ident[:])
                    pe.transpose(bank[:, 5, 384:416], wgt[0:TS, Z2:Z2 + P], ident[0:TS, 0:TS])
                    pe.transpose(bank[:, 5, 416:448], wgt[0:TS, Z2 + P:Z2 + 2 * P], ident[0:TS, 0:TS])
                    pe.transpose(bank[0:TS, 5, 448:480], wgt[0:TS, Z2 + PAST:ZW], ident[0:TS, 0:TS]).then_inc(wT_ready, 1)
                if cur:
                    proj(c, 3, not prev)
                if prev:
                    pe.wait_ge(vn_copied, c * 2)
                    pe.wait_ge(wT_copied, c * 2)
                    pe.wait_ge(cv_landed, c * 16)
                    pe.matmul(bank[:, 6, 0:P], v_nat[:, 0, :], wT[:, 0:P], start=True, stop=True)
                    for t in range(2):
                        pe.matmul(bank[:, 6, P:TP], v_nat[:, t, :], wT[:, (1 + t) * P:(2 + t) * P], start=(t == 0), stop=(t == 1))
                    for t in range(2):
                        pe.matmul(bank[:, 6, TP:T], cv[:, t, :], wT[:, 384 + 32 * t:416 + 32 * t], start=(t == 0), stop=False)
                    pe.matmul(bank[:, 6, TP:T], v_nat[0:TS, 2, :], wT[0:TS, 448:480], start=False, stop=True).then_inc(a_ready, 1)
                if cur:
                    bu(c, 3, False)
                    y_out(c, 2)

            chunk(0, True, False, True)
            chunk(1, True, True, True)
            with pe.Fori(2, NCH) as c:
                chunk(c, True, True, False)
            chunk(LAST_C, False, True, False)

            pe.wait_ge(asq_ready, 1)
            pe.wait_ge(y_read, NCH)
            dense(bank[:, 4, 0:T], lambda k: ones[:], sq, NCH).then_inc(ass_ready, 1)
            pe.wait_ge(a_copied, NCH)
            pe.wait_ge(h_ready, NJ)
            pe.wait_ge(last_ready, NJ)
            for f in range(4):
                mm = pe.transpose(bank[0:NJ, 6, f * P:(f + 1) * P], last[:, f // 2, f % 2, :], ident[:])
            mm.then_inc(lastT_ready, 1)
            pe.wait_ge(z_done, NCH)
            pe.wait_ge(proj_copied, 4 * NCH)
            for m in range(NCH):
                s = m // 2
                if m % 2 == 0:
                    pe.wait_ge(w_landed[s], 16 * (NCH + 1))
                if m >= 2:
                    pe.wait_ge(glu_sig, m - 1)
                w = w_ring[:, s, :].rearrange("p (k n) -> p k n", n=2 * P)
                dense(bank[:, m % 2, 0:T], lambda k: w[:, k, (m % 2) * P:(m % 2 + 1) * P], zT, NCH).then_inc(dense_done, 1)
            pe.wait_ge(wT_copied, 2 * NCH)
            for m in range(NCH):
                pe.wait_ge(ssq_ready, m + 1)
                mm = pe.matmul(bank[:, 5, 0:T], ones[:], sq[:, m], start=(m == 0), stop=(m == NCH - 1))
            mm.then_inc(sss_ready, 1)
            pe.wait_ge(merged_a, NCH)
            pe.wait_ge(merged_s, NCH)
            pe.wait_ge(bu_used, NJ)

            def out_group(i, first):
                for s in range(4):
                    pe.wait_ge(w_landed[s], i * 16 + 16 * (NCH + 2))
                    if not first:
                        pe.wait_ge(res_ready, i * 4 + (s - 3))
                    w = w_ring[:, s, :].rearrange("p (k n) -> p k n", n=P)
                    dense(bank[:, s, 0:T], lambda k: w[:, k, :], mergedT, KC).then_inc(dense_done, 1)

            out_group(0, True)
            with pe.Fori(1, KC // 4) as i:
                out_group(i, False)
            pe.wait_ge(res_ready, KC)
            pe.wait_ge(ms_ready, 2)
            pe.wait_ge(last_copied, 1)
            for t, (t0, m) in enumerate(TT):
                if t >= 2:
                    pe.wait_ge(xh_ready, t - 1)
                for k in range(KC):
                    mm = pe.transpose(bank[0:m, 4 * (t % 2) + k // 4, (k % 4) * P:(k % 4 + 1) * P], xT[:, k, t0:t0 + m], ident[:])
                mm.then_inc(nat_ready, 1)
            for t, (t0, m) in enumerate(TT):
                pe.wait_ge(h_rows_ready, t + 1)
                pe.wait_ge(xh_ready, (2, 3, 3)[t])
                for q in range(4):
                    if t == 2:
                        pe.wait_ge(hT_copied, q + 1)
                    for k in range(4):
                        mm = pe.transpose(bank[:, (4, 0, 4)[t] + q, k * m:(k + 1) * m], rows[0:m, t, (4 * q + k) * P:(4 * q + k + 1) * P], ident[0:m, 0:m])
                    mm.then_inc(hT_ready, 1)
            for t, (t0, m) in enumerate(TT):
                pe.wait_ge(hT_copied, 4 * max(t, 1) + 4)
                if t == 0:
                    pe.wait_ge(router_landed, 64)
                for k in range(KC):
                    mm = pe.matmul(bank[0:m, 0, t * RW:(t + 1) * RW], hT[:, k, t0:t0 + m], w_router[:, k, :], start=(k == 0), stop=(k == KC - 1))
                mm.then_inc(logits_ready, 1)
            pe.wait_ge(pick_ready, 1)
            pe.matmul(bank[:, 1, 0:NE], upper[:], pick[:, 0, :], start=True, stop=True)
            pe.matmul(bank[:, 1, NE:2 * NE], ones[:], pick[:, 0, :], start=True, stop=False)
            pe.matmul(bank[:, 1, NE:2 * NE], upper[:], pick[:, 1, :], start=False, stop=True)
            for out, lhs2, m in ((bank[0:TS, 1, 2 * NE:3 * NE], upper[0:TS, 0:TS], TS), (bank[:, 1, 3 * NE:4 * NE], ones[0:TS, :], P)):
                pe.matmul(out, ones[:, 0:m], pick[:, 0, :], start=True, stop=False)
                pe.matmul(out, ones[:, 0:m], pick[:, 1, :], start=False, stop=False)
                mm = pe.matmul(out, lhs2, pick[0:TS, 2, :], start=False, stop=True)
            mm.then_inc(rank_ready, 1)

            def x_turn(b):
                pe.wait_ge(xe_landed, b * 32 + 32)
                for c in range(KC // 2):
                    mm = pe.transpose(bank[:, 1 + c // 4, (c % 4) * P:(c % 4 + 1) * P], x_exp[:, c * P:(c + 1) * P], ident[:])
                mm.then_inc(xeT_ready, 1)

            def expert(b, first, middle=None):
                pe.wait_ge(xeT_act, b + 1)
                pe.wait_ge(xeT_dve, b + 1)
                gu = bank[:, 0, :].rearrange("p (g n) -> p g n", g=2)
                for s in range(8):
                    pe.wait_ge(ew_landed[s], b * 16 + 16)
                    w = e_ring[:, s, :].rearrange("p (k f) -> p k f", k=4)
                    for kk in range(4):
                        k = 4 * (s // 2) + kk
                        for h in range(2):
                            mm = pe.matmul(gu[h * B:(h + 1) * B, s % 2, :], xT_exp[:, k % 8, k // 8, :], w[:, kk, h * FH:(h + 1) * FH],
                                           start=(s == 0 and kk == 0), stop=(k == KC - 1), skip_group_check=True)
                    mm.then_inc(ew_used, 1)
                x_turn(b + 1)
                if middle is not None:
                    middle()
                pe.wait_ge(hid_ready, b + 1)
                for c in range(2):
                    mm = pe.transpose(bank[:, 5, c * P:(c + 1) * P], hid[:, c * P:(c + 1) * P], ident[:])
                mm.then_inc(hidT_ready, 1)
                pe.wait_ge(hidT_copied, b + 1)
                if not first:
                    pe.wait_ge(ye_act, b)
                    pe.wait_ge(ye_dve, b)
                for j in range(FC):
                    pe.wait_ge(ew_landed[8 + j], b * 16 + 16)
                    for n in range(2):
                        for h in range(2):
                            mm = pe.matmul(bank[h * B:(h + 1) * B, 3 + n, :], hidT[:, j % 2, j // 2, :],
                                           e_ring[:, 8 + j, h * DH2 + n * 512:h * DH2 + (n + 1) * 512],
                                           start=(j == 0), stop=(j == FC - 1))
                    mm.then_inc(ew_used, 1)

            def pair(i, first):
                def ple_gate():
                    pe.wait_ge(w_landed[0], i * 16 + 16 * (NCH + 2 + KC // 4))
                    if not first:
                        pe.wait_ge(ple_mul, i)
                    w = w_ring[:, 0, :].rearrange("p (k n) -> p k n", n=P)
                    dense(bank[:, 7, 0:T], lambda k: w[:, k, :], hT, KC).then_inc(dense_done, 1)

                def ple_proj():
                    pe.wait_ge(w_landed[1], i * 16 + 16 * (NCH + 2 + KC // 4))
                    pe.wait_ge(plg_sig, i + 1)
                    w = w_ring[:, 1, 0:PLC * P].rearrange("p (k n) -> p k n", n=P)
                    dense(bank[:, 7, 0:T], lambda k: w[:, k, :], pT, PLC).then_inc(dense_done, 1)

                expert(i * 2, first, ple_gate)
                expert(i * 2 + 1, False, ple_proj)

            pe.wait_ge(idx_ready, 1)
            x_turn(0)
            pair(0, True)
            with pe.Fori(1, NE // 2) as i:
                pair(i, False)
            further_blocks(pe, lambda i: expert(i + NE, False))
            pe.wait_ge(ple_done, KC)
            pe.wait_ge(all_stored, 1)
            for t, (t0, m) in enumerate(TT):
                if t >= 2:
                    pe.wait_ge(fin_sum, t - 1)
                for k in range(KC):
                    mm = pe.transpose(bank[0:m, 4 * (t % 2) + k // 4, (k % 4) * P:(k % 4 + 1) * P], accT[:, k, t0:t0 + m], ident[:])
                mm.then_inc(fin_nat, 1)

        @block.vector
        def _(dve):
            own = OwnOrder(dve, dve_own)
            TWO_PI = 2.0 * math.pi
            PI_IN = 3.1415925
            PI_HI, ROUND = 6.28125, 12582912.0
            own(dve.memset(zero_col[:], 0.0))
            own(dve.memset(var_eps[:], 1.0))
            own(dve.memset(later, 1.0))
            own(dve.memset(tab_f[:], 0.0))

            def row_stats(t, m, src):
                for q in range(4):
                    own(dve.bn_stats(stats[0:m, t, q, :], src(q)))
                own.wait()
                own(dve.bn_aggr(mean_var[0:m, t, :], stats[0:m, t].rearrange("p q s -> p (q s)")))
                own.wait()
                return dve.tensor_scalar(var_eps[0:m, t:t + 1], mean_var[0:m, t, 1:2], LN_EPS, None, ALU.add)

            dve.wait_ge(x_landed, 16 * NT)
            own.wait()
            for t, (_, m) in enumerate(TT):
                row_stats(t, m, lambda q: rows[0:m, t, q * 512:(q + 1) * 512]).then_inc(var_ready, 1)
            dve.wait_ge(rstd_ready, 1)
            for t, (_, m) in enumerate(TT):
                dve.tensor_scalar(rows[0:m, t, :], rows[0:m, t, :], mean_var[0:m, t, 0:1], rstd[0:m, t:t + 1],
                                  ALU.subtract, ALU.mult).then_inc(xn_ready, 1)

            def f(i, j=None):
                return pr[:, i, :] if j is None else pr[:, i:j, :]

            def halves(i):
                return f(i).rearrange("j (a s) -> j a s", a=2)

            dve.wait_ge(small_landed, 80)
            dve.wait_ge(pr_act_out, 1)
            own(dve.tensor_scalar(f(0), f(0), -1e-4, None, ALU.min))
            own.wait()
            step = pr[:, 4, 2:4].unsqueeze(2).to_broadcast([NJ, 2, NS])
            own(dve.tensor_tensor(halves(5), halves(0), step, ALU.mult))
            own(dve.tensor_tensor(halves(6), halves(1), step, ALU.mult))
            own.wait()
            own(dve.tensor_scalar(f(7), f(6), 1.0 / TWO_PI, ROUND, ALU.mult, ALU.add))
            own.wait()
            own(dve.tensor_scalar(f(7), f(7), -ROUND, None, ALU.add))
            own.wait()
            own(dve.scalar_tensor_tensor(out=f(13), in0=f(7), scalar=-PI_HI, in1=f(6), op0=ALU.mult, op1=ALU.add))
            own.wait()
            own(dve.scalar_tensor_tensor(out=f(12), in0=f(7), scalar=-(TWO_PI - PI_HI), in1=f(13), op0=ALU.mult, op1=ALU.add))
            own.wait()
            own(dve.tensor_scalar(f(13), f(12), math.pi / 2, -TWO_PI, ALU.is_gt, ALU.mult))
            own.wait()
            own(dve.scalar_tensor_tensor(out=f(11), in0=f(12), scalar=math.pi / 2, in1=f(13), op0=ALU.add, op1=ALU.add))
            own.wait()
            dve.tensor_scalar(f(11, 13), f(11, 13), -PI_IN, PI_IN, ALU.max, ALU.min).then_inc(pr_act_in, 1)
            dve.wait_ge(vecT_copied, 1)
            for k in range(1, KC, 2):
                dve.wait_ge(xt_ready, k + 1)
                a, b = vec_at["ln_in_g"] + k, vec_at["ln_in_b"] + k
                dve.tensor_scalar(xT[:, k, :], bank[:, k % 4, 0:T], vecT[:, a:a + 1], vecT[:, b:b + 1],
                                  ALU.mult, ALU.add).then_inc(xt_odd, 1)
            dve.wait_ge(pr_act_out, 3)
            own(dve.tensor_tensor(f(13), f(8), f(9), ALU.mult))
            own(dve.tensor_tensor(f(14), f(8), f(10), ALU.mult))
            own(dve.tensor_tensor(f(15), f(0), f(0), ALU.mult))
            own(dve.tensor_tensor(f(7), f(1), f(1), ALU.mult))
            own.wait()
            own(dve.tensor_scalar(f(13), f(13), -1.0, None, ALU.add))
            own(dve.tensor_tensor(f(15), f(15), f(7), ALU.add))
            own.wait()
            own(dve.reciprocal(f(15), f(15)))
            own(dve.tensor_tensor(f(16), f(13), f(0), ALU.mult))
            own(dve.tensor_tensor(f(17), f(14), f(1), ALU.mult))
            own(dve.tensor_tensor(f(5), f(14), f(0), ALU.mult))
            own(dve.tensor_tensor(f(6), f(13), f(1), ALU.mult))
            own.wait()
            own(dve.tensor_tensor(f(16), f(16), f(17), ALU.add))
            own(dve.tensor_tensor(f(5), f(5), f(6), ALU.subtract))
            own.wait()
            own(dve.tensor_tensor(f(16), f(16), f(15), ALU.mult))
            dve.tensor_tensor(f(17), f(5), f(15), ALU.mult).then_inc(pr_ready, 1)
            dve.wait_ge(par_copied, 1)
            dve.wait_ge(masks_ready, 1)
            own(dve.tensor_scalar(coef[:, :, :, 0], par[:, 3:5, :], par_b[:, 0:1], None, ALU.mult))
            own.wait()
            dve.tensor_scalar(coef[:, :, :, 1], par[:, 3:5, :], par_b[:, 1:2], None, ALU.mult).then_inc(coef_ready, 1)

            def tile(c, i, first):
                n = c * JC + i
                cb = 0 if first else c % 2
                w = tb[:, ds(cb, 1), :, i, :].rearrange("p b r t -> p (b r) t")
                wre, wim = (w[:, r:r + 1, :].to_broadcast([P, 2, T]) for r in range(2))
                dve.wait_ge(bu_ready, n + 1)
                own(dve.tensor_tensor(tmp1, bank[:, 2:4, 0:T], wre, ALU.mult))
                dve.tensor_tensor(tmp2, bank[:, 2:4, 0:T], wim, ALU.mult).then_inc(bu_used, 1)
                dve.wait_ge(bu_used, n + 1)
                own(dve.tensor_tensor(rot[:, 0, :], tmp1[:, 0, :], tmp2[:, 1, :], ALU.add))
                own(dve.tensor_tensor(rot[:, 1, :], tmp1[:, 1, :], tmp2[:, 0, :], ALU.subtract))
                own.wait()
                for r in range(2):
                    for a, b, start in ((0, TP, 0.0), (TP, T, par_c[:, 5 + r, i:i + 1])):
                        own(dve.tensor_tensor_scan(scan[:, r, a:b], par_c[:, 0, i:i + 1].to_broadcast([P, b - a]),
                                                   rot[:, r, a:b], start, ALU.mult, ALU.add))
                own.wait()
                own(dve.tensor_tensor(tmp1, scan, wre, ALU.mult))
                own(dve.tensor_tensor(tmp2, scan, wim, ALU.mult))
                own.wait()
                if not (first and i < 2):
                    dve.wait_ge(y_part, n - 1)
                own(dve.tensor_tensor(h_ssm[:, i % 2, 0, :], tmp1[:, 0, :], tmp2[:, 1, :], ALU.subtract))
                dve.tensor_tensor(h_ssm[:, i % 2, 1, :], tmp1[:, 1, :], tmp2[:, 0, :], ALU.add).then_inc(h_ready, 1)
                dve.wait_ge(h_ready, n + 1)
                dve.tensor_copy(last[:, :, :, ds(n, 1)].rearrange("p r t j -> p r (t j)"),
                                h_ssm[:, i % 2, :, TP - 1:T:TS]).then_inc(last_ready, 1)

            def chunk(c, cur, prev, first):
                if prev:
                    dve.wait_ge(z_ready, c)
                    own(dve.scalar_tensor_tensor(out=zm[:, 0:Z2], in0=bank[:, 5, 0:Z2], scalar=SCALE, in1=mask,
                                                 op0=ALU.mult, op1=ALU.add))
                    dve.scalar_tensor_tensor(out=zm[0:TS, Z2:ZW], in0=bank[0:TS, 6, 0:PAST + TS], scalar=SCALE,
                                             in1=mask_s[0:TS], op0=ALU.mult, op1=ALU.add).then_inc(zm_ready, 1)
                    dve.wait_ge(y_part, c * JC)
                    dve.tensor_tensor(yT, bank[:, 4, 0:T], du, ALU.add).then_inc(y_read, 1)
                    dve.wait_ge(y_read, c)
                    own(dve.tensor_tensor(y2, yT, yT, ALU.mult))
                    own.wait()
                    dve.scalar_tensor_tensor(out=y2, in0=y2, scalar=1.0 / 0.044715, in1=yT, op0=ALU.add,
                                             op1=ALU.mult).then_inc(gelu_in, 1)
                if cur:
                    own(dve.tensor_copy(par_c, par[:, :, ds(c * JC, JC)]))
                    own(dve.tensor_copy(d_c, vecT[:, ds(c + vec_at["ssm_d"], 1)]))
                    own.wait()
                    dve.wait_ge(proj_copied, c * 4 + 1)
                    dve.tensor_scalar(du, uT, d_c, None, ALU.mult).then_inc(du_ready, 1)
                    dve.wait_ge(table_ready, c + 1)
                    tile(c, 0, not prev)
                if prev:
                    dve.wait_ge(sig_ready, c)
                    if not first:
                        dve.wait_ge(wT_ready, c - 1)
                    segs = ((P, 0, P, 0), (P, Z1, TP, Z1 + 1), (TS, Z2, PAST + TS, Z2 + 2))
                    for m, z0, n, l0 in segs:
                        own(dve.tensor_tensor_scan(later[0:m, l0:l0 + n][:, ::-1], keep[0:m, z0:z0 + n][:, ::-1],
                                                   zero_col[0:m, 0:1].to_broadcast([m, n]), 1.0, ALU.mult, ALU.add))
                    own.wait()
                    for k, (m, z0, n, l0) in enumerate(segs):
                        v = dve.tensor_tensor(wgt[0:m, z0:z0 + n], sig[0:m, z0:z0 + n], later[0:m, l0 + 1:l0 + 1 + n], ALU.mult)
                        if k == 2:
                            v.then_inc(wgt_ready, 1)
                    dve.wait_ge(gelu_sig, c)
                    dve.tensor_tensor(zT[:, ds(c - 1, 1), :].rearrange("p a t -> p (a t)"), yT, ysig, ALU.mult).then_inc(z_done, 1)
                if cur:
                    for i in range(1, JC):
                        tile(c, i, not prev)

            chunk(0, True, False, True)
            chunk(1, True, True, True)
            base = own.base + own.n
            with dve.Fori(2, NCH) as c:
                own.enter((c - 2) * DVE_PER_CHUNK + base)
                chunk(c, True, True, False)
                assert own.n == DVE_PER_CHUNK, own.n
            own.enter(base + (NCH - 2) * DVE_PER_CHUNK)
            chunk(LAST_C, False, True, False)

            def merge(i, n0, src, name, done):
                dve.wait_ge(rms_root, i + 1)
                r = (rms_a, rms_s)[i]
                dve.reciprocal(r, r).then_inc(rms_ready, 1)
                dve.wait_ge(rms_ready, i + 1)
                for m in range(NCH):
                    a = vec_at[name] + m
                    dve.scalar_tensor_tensor(out=mergedT[:, n0 + m, :], in0=src[:, m], scalar=vecT[:, a:a + 1],
                                             in1=r, op0=ALU.mult, op1=ALU.mult).then_inc(done, 1)

            dve.wait_ge(ass_ready, 1)
            dve.tensor_scalar(rms_a, bank[:, 4, 0:T], 1.0 / W, LN_EPS, ALU.mult, ALU.add).then_inc(ms_ready, 1)
            dve.wait_ge(a_copied, NCH)
            merge(0, 0, attnT, "g_attn", merged_a)
            dve.wait_ge(z_done, NCH)
            for m in range(NCH):
                dve.wait_ge(glu_sig, m + 1)
                dve.tensor_tensor(ssmT[:, m], zT[:, m], sg[:, m % 2], ALU.mult).then_inc(s_ready, 1)
            dve.wait_ge(sss_ready, 1)
            dve.tensor_scalar(rms_s, bank[:, 5, 0:T], 1.0 / W, LN_EPS, ALU.mult, ALU.add).then_inc(ms_ready, 1)
            merge(1, NCH, ssmT, "g_ssm", merged_s)

            with dve.Fori(0, KC // 4) as i:
                for s in range(4):
                    dve.wait_ge(dense_done, i * 4 + (N_OUT + s + 1))
                    v = xT[:, ds(i * 4 + s, 1), :].rearrange("p a t -> p (a t)")
                    dve.scalar_tensor_tensor(out=v, in0=v, scalar=ALPHA, in1=bank[:, s, 0:T], op0=ALU.mult,
                                             op1=ALU.add).then_inc(res_ready, 1)

            def neg_mean_of(t, m):
                return dve.scalar_tensor_tensor(out=neg_mean[0:m, t:t + 1], in0=mean_var[0:m, t, 0:1], scalar=-1.0,
                                                in1=rstd[0:m, t:t + 1], op0=ALU.mult, op1=ALU.mult)

            def ln1_gain(t, m):
                dve.wait_ge(xh_ready, t + 1)
                dve.tensor_tensor(rows[0:m, t, :], rows[0:m, t, :], w_ring[0:m, 2, :], ALU.mult).then_inc(hg_ready, 1)

            own(dve.memset(logits, 0.0))
            for t, (_, m) in enumerate(TT):
                dve.wait_ge(nat_ready, t + 1)
                row_stats(t, m, lambda q: bank[0:m, 4 * (t % 2) + q, :]).then_inc(var1_ready, 1)
                dve.wait_ge(rstd1_ready, t + 1)
                neg_mean_of(t, m).then_inc(nm1_ready, 1)
                if t == 0:
                    dve.wait_ge(gb1_landed, 32)
                if t:
                    ln1_gain(t - 1, P)
            ln1_gain(NT - 1, TS)

            dve.wait_ge(logits_ready, NT)
            for t, (_, m) in enumerate(TT):
                own(dve.tensor_tensor(logits[0:m, t, :], bank[0:m, 0, t * RW:(t + 1) * RW], b_router[0:m, :], ALU.add))
            own.wait()

            def bc(v, n):
                return v.unsqueeze(2).to_broadcast([P, NT, n])

            def iob(n):
                return io[:, 0:n].unsqueeze(1).to_broadcast([P, NT, n])

            def first_max(v, n, hot, best):
                own(dve.tensor_reduce(best, v, AX_X, ALU.max))
                own.wait()
                own(dve.tensor_tensor(hot, v, bc(best, n), ALU.is_equal))
                own.wait()
                own(dve.scalar_tensor_tensor(out=hot, in0=hot, scalar=-64.0, in1=iob(n), op0=ALU.mult, op1=ALU.add))
                own.wait()
                own(dve.tensor_reduce(r_low, hot, AX_X, ALU.min))
                own.wait()
                own(dve.tensor_tensor(hot, hot, bc(r_low, n), ALU.is_equal))
                own.wait()

            gl = logits[:, :, 0:NGRP]
            first_max(gl, NGRP, g_hot, r_max)
            own(dve.tensor_tensor(d5[:, :, 0:NGRP], gl, bc(r_max, NGRP), ALU.subtract))
            own(dve.tensor_scalar(g_hot, g_hot, -1.0, -NEG, ALU.add, ALU.mult))
            own.wait()
            own(dve.tensor_tensor(el.rearrange("p t (g x) -> p t g x", g=NGRP),
                                  logits[:, :, NGRP:RW].rearrange("p t (g x) -> p t g x", g=NGRP),
                                  g_hot.unsqueeze(3).to_broadcast([P, NT, NGRP, EPG]), ALU.add))
            own.wait()
            first_max(el, NE, pick1, top1)
            own(dve.scalar_tensor_tensor(out=el, in0=pick1, scalar=NEG, in1=el, op0=ALU.mult, op1=ALU.add))
            own.wait()
            first_max(el, NE, pick2, top2)
            dve.tensor_tensor(pick, pick1, pick2, ALU.add).then_inc(pick_ready, 1)
            dve.tensor_tensor(d5[:, :, NGRP], top2, top1, ALU.subtract).then_inc(exp_in, 1)
            dve.wait_ge(exp_out, 1)
            own(dve.tensor_reduce(top1, e5[:, :, 0:NGRP], AX_X, ALU.add))
            own(dve.memset(counts, 0.0))
            own.wait()
            own(dve.scalar_tensor_tensor(out=top1, in0=e5[:, :, NGRP], scalar=1.0, in1=top1, op0=ALU.add, op1=ALU.mult))
            own.wait()
            own(dve.reciprocal(gate1[:], top1))
            own.wait()
            own(dve.tensor_tensor(gate2[:], gate1[:], e5[:, :, NGRP], ALU.mult))
            dve.wait_ge(rank_ready, 1)
            own(dve.tensor_copy(counts[:, 0:2 * NE], bank[:, 1, 0:2 * NE]))
            own(dve.tensor_copy(counts[0:TS, 2 * NE:3 * NE], bank[0:TS, 1, 2 * NE:3 * NE]))
            own(dve.tensor_copy(counts[:, 3 * NE:4 * NE], bank[:, 1, 3 * NE:4 * NE]))
            own.wait()
            cnt = counts[:, 3 * NE:4 * NE]
            zb = zero_col[:, 0:1].to_broadcast([P, NE])
            rank = counts[:, 0:3 * NE].rearrange("p (t e) -> p t e", t=NT)

            def over_tiles(v):
                return v.unsqueeze(1).to_broadcast([P, NT, NE])

            own(dve.tensor_tensor_scan(first_row, cnt, zb, 0.0, ALU.add, ALU.add))
            own(dve.tensor_scalar(more, cnt, float(B), None, ALU.is_gt))
            own.wait()
            own(dve.tensor_tensor(first_row, first_row, cnt, ALU.subtract))
            for k in range(2, MB):
                own(dve.scalar_tensor_tensor(out=more, in0=cnt, scalar=float(B * k), in1=more, op0=ALU.is_gt, op1=ALU.add))
                own.wait()
            own(dve.tensor_tensor_scan(more_at, more, zb, 0.0, ALU.add, ALU.add))
            own.wait()
            own(dve.tensor_tensor(more_at, more_at, more, ALU.subtract))
            own.wait()
            own(dve.scalar_tensor_tensor(out=jump, in0=more_at, scalar=float(NE - 1), in1=io[:], op0=ALU.add, op1=ALU.subtract))
            own(dve.tensor_tensor(place, rank, over_tiles(first_row), ALU.add))
            own.wait()

            def sum_picked(k, pk):
                own(dve.tensor_tensor(picked, pk, place, ALU.mult))
                own.wait()
                own(dve.tensor_reduce(sums[:, k, :], picked, AX_X, ALU.add))
                own.wait()

            sum_picked(0, pick1)
            sum_picked(1, pick2)
            own(dve.scalar_tensor_tensor(out=place, in0=rank, scalar=float(B), in1=over_tiles(jump), op0=ALU.is_ge, op1=ALU.mult))
            own.wait()
            own(dve.tensor_tensor(place, place, over_tiles(io[:]), ALU.add))
            own.wait()
            own(dve.scalar_tensor_tensor(out=place, in0=place, scalar=float(B), in1=rank, op0=ALU.mult, op1=ALU.add))
            own.wait()
            sum_picked(2, pick1)
            sum_picked(3, pick2)
            dve.tensor_copy(idx[:], sums[:]).then_inc(idx_ready, 1)
            fr, mr, ma = first_row[0:1, :], more[0:1, :], more_at[0:1, :]
            o = [v.rearrange("p (i e) -> p i e", e=NE) for v in ov]
            ib = io[0:1, 0:NOV].unsqueeze(2).to_broadcast([1, NOV, NE])

            def blocks(v):
                return v.unsqueeze(1).to_broadcast([1, NOV, NE])

            j1 = jump[0:1, :]
            own(dve.tensor_tensor(o[0], blocks(ma), ib, ALU.is_le))
            own(dve.tensor_tensor(j1, ma, mr, ALU.add))
            own.wait()
            own(dve.tensor_tensor(o[1], blocks(j1), ib, ALU.is_gt))
            own(dve.tensor_copy(tab_f[0:1, NTAB + NOV:NTAB + NOV + 1], jump[0:1, NE - 1:NE]))
            own.wait()
            own(dve.tensor_tensor(o[0], o[0], o[1], ALU.mult))
            own(dve.scalar_tensor_tensor(out=j1, in0=ma, scalar=-float(B), in1=fr, op0=ALU.mult, op1=ALU.add))
            own.wait()
            own(dve.tensor_scalar(j1, j1, float(B), None, ALU.add))
            own(dve.tensor_tensor(o[1], o[0], blocks(io[0:1, :]), ALU.mult))
            own.wait()
            own(dve.tensor_tensor(o[2], o[0], blocks(j1), ALU.mult))
            own(dve.tensor_reduce(tab_f[0:1, NTAB:NTAB + NOV], o[1], AX_X, ALU.add))
            own.wait()
            own(dve.tensor_reduce(sums_ov[0:1, :], o[2], AX_X, ALU.add))
            own(dve.tensor_reduce(in_use[0:1, :], o[0], AX_X, ALU.add))
            own(dve.tensor_copy(tab_f[0:1, 0:NE], fr))
            own.wait()
            own(dve.tensor_tensor(in_use[0:1, :], in_use[0:1, :], io[0:1, 0:NOV], ALU.mult))
            own.wait()
            own(dve.scalar_tensor_tensor(out=tab_f[0:1, NE:NE + NOV], in0=in_use[0:1, :], scalar=float(B),
                                         in1=sums_ov[0:1, :], op0=ALU.mult, op1=ALU.add))
            own.wait()
            dve.tensor_copy(tab[:], tab_f[:]).then_inc(tab_ready, 1)
            dve.wait_ge(tab_ready, 1)

            def x_copy(b):
                dve.wait_ge(xeT_ready, b + 1)
                dve.tensor_copy(xT_exp[:, 4:8].rearrange("p k h n -> p (k h n)"), bank[:, 2, :]).then_inc(xeT_dve, 1)

            def expert(b, first, middle=None):
                dve.wait_ge(gsig_ready, b + 1)
                dve.tensor_tensor(hid[:], bank[:, 0, 0:FH], sig_exp[:], ALU.mult).then_inc(gmul_ready, 1)
                dve.wait_ge(gmul_ready, b + 1)
                dve.tensor_tensor(hid[:], hid[:], bank[:, 0, FH:FE], ALU.mult).then_inc(hid_ready, 1)
                x_copy(b + 1)
                dve.wait_ge(hidT_ready, b + 1)
                dve.tensor_copy(hidT[:].rearrange("p c h n -> p (c h n)"), bank[:, 5, 0:FC * B]).then_inc(hidT_copied, 1)
                if middle is not None:
                    middle()
                dve.wait_ge(ew_used, b * NEW + NEW)
                if not first:
                    dve.wait_ge(ye_stored, b * 32)
                dve.tensor_copy(y_exp[:, 512:DH2], bank[:, 4, :]).then_inc(ye_dve, 1)

            def pair(i, first):
                def ple():
                    dve.wait_ge(dense_done, i * 2 + (N_PLE + 2))
                    dve.wait_ge(plg_sig, i + 1)
                    if not first:
                        dve.wait_ge(ple_done, i)
                    dve.tensor_tensor(ple_tmp[:], ple_sig[:], bank[:, 7, 0:T], ALU.mult).then_inc(ple_mul, 1)
                    dve.wait_ge(ple_mul, i + 1)
                    v, h = (u[:, ds(i, 1), :].rearrange("p a t -> p (a t)") for u in (accT, hT))
                    dve.scalar_tensor_tensor(out=v, in0=h, scalar=ALPHA, in1=ple_tmp[:], op0=ALU.mult, op1=ALU.add).then_inc(ple_done, 1)
                expert(i * 2, first)
                expert(i * 2 + 1, False, ple)

            x_copy(0)
            pair(0, True)
            with dve.Fori(1, NE // 2) as i:
                pair(i, False)
            further_blocks(dve, lambda i: expert(i + NE, False))

            dve.wait_ge(gb2_landed, 32)
            for t, (_, m) in enumerate(TT):
                dve.wait_ge(y_gathered[t], 32)
                dve.wait_ge(fin_nat, t + 1)
                b0 = 4 * (t % 2)
                s = e_ring[0:m, t, :]
                dve.scalar_tensor_tensor(out=s, in0=s, scalar=gate1[0:m, t:t + 1],
                                         in1=bank[0:m, b0:b0 + 4, :].rearrange("p b n -> p (b n)"),
                                         op0=ALU.mult, op1=ALU.add).then_inc(fin_sum, 1)
                dve.wait_ge(fin_sum, t + 1)
                own(dve.scalar_tensor_tensor(out=s, in0=e_ring[0:m, NT + t, :], scalar=gate2[0:m, t:t + 1], in1=s,
                                             op0=ALU.mult, op1=ALU.add))
                own.wait()
                row_stats(t, m, lambda q: e_ring[0:m, t, q * 512:(q + 1) * 512]).then_inc(fin_var, 1)
                dve.wait_ge(fin_rstd, t + 1)
                neg_mean_of(t, m).then_inc(fin_nm, 1)
                if t:
                    dve.wait_ge(fin_xh, t)
                    v = e_ring[0:P, t - 1, :]
                    dve.tensor_tensor(v, v, w_ring[0:P, 2, :], ALU.mult).then_inc(fin_g, 1)
            dve.wait_ge(fin_xh, NT)
            v = e_ring[0:TS, NT - 1, :]
            dve.tensor_tensor(v, v, w_ring[0:TS, 2, :], ALU.mult).then_inc(fin_g, 1)


_INS = ['x_prompt', 'x_sample', 'p_prompt', 'p_sample', 'cache_k', 'cache_v', 'state_ssm_re', 'state_ssm_im',
        'ln_in_g', 'ln_in_b', 'w_in', 'ssm_lam_re', 'ssm_lam_im', 'ssm_log_step', 'ssm_b_re', 'ssm_b_im',
        'ssm_c_re', 'ssm_c_im', 'ssm_d', 'ssm_w_glu', 'ssm_b_glu', 'g_attn', 'g_ssm', 'w_out', 'ln1_g', 'ln1_b',
        'w_router_group', 'b_router_group', 'w_router_expert', 'b_router_expert',
        'w_exp_gate', 'w_exp_up', 'w_exp_down', 'w_ple_gate', 'w_ple_proj', 'ln2_g', 'ln2_b']
_OUTS = [(1, 256, 2048), (1, 32, 2048), (1, 1, 256, 8, 128), (1, 1, 256, 8, 128), (1, 1, 64, 64), (1, 1, 64, 64),
         (1, 1, 32, 8, 128), (1, 1, 32, 8, 128), (1, 1, 64, 64), (1, 1, 64, 64)]


def kernel(**inputs):
    import numpy as _np
    import concourse.bacc as _bacc
    from concourse import mybir as _mybir
    from concourse.bass_utils import run_bass_kernel_spmd as _run

    nc = _bacc.Bacc("TRN2", target_bir_lowering=False, num_devices=1)
    arrays, args = {}, []
    for name in _INS:
        a = _np.ascontiguousarray(inputs[name])
        arrays[f"in_{name}_dram"] = a
        args.append(nc.dram_tensor(f"in_{name}_dram", a.shape, _mybir.dt.from_np(a.dtype), kind="ExternalInput").ap())
    for i, shape in enumerate(_OUTS):
        args.append(nc.dram_tensor(f"out_{i}_dram", shape, _mybir.dt.float32, kind="ExternalOutput").ap())
    build(nc, *args)
    r = _run(nc, [arrays], core_ids=[0])
    return tuple(r.results[0][f"out_{i}_dram"] for i in range(len(_OUTS)))
```

```python
import math
from contextlib import ExitStack

import concourse.bass as bass
from concourse import mybir

P = 128
POOL_PER_PAIR = 84
DVE_PER_CHUNK = 47
F32 = mybir.dt.float32
I32 = mybir.dt.int32
ALU = mybir.AluOpType
ACT = mybir.ActivationFunctionType
AX_X = mybir.AxisListType.X
ds = bass.ds


class OwnOrder:

    def __init__(self, eng, sem):
        self.eng, self.sem, self.base, self.n = eng, sem, 0, 0

    def __call__(self, ins):
        self.n += 1
        return ins.then_inc(self.sem, 1)

    def wait(self):
        self.eng.wait_ge(self.sem, self.base + self.n)

    def enter(self, base):
        self.base, self.n = base, 0


def build(nc, x_prompt, x_sample, p_prompt, p_sample, cache_k, cache_v, state_ssm_re, state_ssm_im,
          ln_in_g, ln_in_b, w_in, ssm_lam_re, ssm_lam_im, ssm_log_step, ssm_b_re, ssm_b_im,
          ssm_c_re, ssm_c_im, ssm_d, ssm_w_glu, ssm_b_glu, g_attn, g_ssm, w_out, ln1_g, ln1_b,
          w_router_group, b_router_group, w_router_expert, b_router_expert,
          w_exp_gate, w_exp_up, w_exp_down, w_ple_gate, w_ple_proj, ln2_g, ln2_b,
          y_prompt, y_sample, k_prompt, v_prompt, ssm_re_prompt, ssm_im_prompt,
          k_sample, v_sample, ssm_re_sample, ssm_im_sample):
    _, TP, D = x_prompt.shape
    TS = x_sample.shape[1]
    T = TP + TS
    KC = D // P
    NH, DH = cache_k.shape[3], cache_k.shape[4]
    PAST = cache_k.shape[2]
    W = NH * DH
    NCH = W // P
    NG, NS = ssm_lam_re.shape[1:]
    GC = ssm_d.shape[2]
    NJ = NG * NS // P
    JC = NJ // NCH
    NE, _, FE = w_exp_gate.shape[1:]
    NGRP = w_router_group.shape[2]
    EPG = NE // NGRP
    FC = FE // P
    PLC = w_ple_proj.shape[1] // P
    LN_EPS = 1e-5
    ALPHA = 2.0 ** 0.25
    SCALE = float(DH) ** -0.5
    NEG = -1e30
    TT = [(0, P), (P, P), (2 * P, TS)]
    NT = len(TT)
    IN_ORDER = (2, 0, 1)
    assert (TP, TS, PAST, DH, JC, P // NS) == (256, 32, 256, P, 4, 2)
    B = 64
    MB = -(-T // B)
    NOV = T * 2 // B
    assert NOV % 3 == 0
    XROWS = 2 * T + B
    YROWS = (NE + NOV) * B
    RW = NGRP + NE

    x_src = [x_prompt[0, 0:P, :], x_prompt[0, P:2 * P, :], x_sample[0]]
    y_dst = [y_prompt[0, 0:P, :], y_prompt[0, P:2 * P, :], y_sample[0]]
    p_src = [p_prompt[0, 0, 0:P, :], p_prompt[0, 0, P:2 * P, :], p_sample[0, 0]]
    w_in_v = w_in[0].rearrange("(k p) n -> p k n", p=P)
    w_glu_v = ssm_w_glu[0].rearrange("(k p) n -> p k n", p=P)
    w_out_v = w_out[0].rearrange("(k p) n -> p k n", p=P)
    w_plg_v = w_ple_gate[0].rearrange("(k p) n -> p k n", p=P)
    w_plp_v = w_ple_proj[0].rearrange("(k p) n -> p k n", p=P)
    ck_v = cache_k[0, 0].rearrange("(t p) h d -> p t h d", p=P)
    cv_v = cache_v[0, 0].rearrange("(t p) h d -> p t h d", p=P)
    kp_v = k_prompt[0, 0].rearrange("(t p) h d -> p t h d", p=P)
    vp_v = v_prompt[0, 0].rearrange("(t p) h d -> p t h d", p=P)
    b_v = [b[0].rearrange("g s n -> (g s) n").rearrange("(c j p) n -> p c j n", j=JC, p=P)
           for b in (ssm_b_re, ssm_b_im)]
    c_v = [c[0].rearrange("g n s -> (g n) s").rearrange("(c p) s -> p c s", p=P) for c in (ssm_c_re, ssm_c_im)]
    rows_v = [a.rearrange("g s -> (g s)").rearrange("(j p) -> j p", p=P)
              for a in (ssm_lam_re[0], ssm_lam_im[0], state_ssm_re[0, 0], state_ssm_im[0, 0])]
    step_v = ssm_log_step[0].rearrange("(j a) -> j a", a=2)
    last_v = [a[0, 0].rearrange("g s -> (g s)").rearrange("(j p) -> j p", p=P)
              for a in (ssm_re_prompt, ssm_re_sample, ssm_im_prompt, ssm_im_sample)]
    wg_v = w_exp_gate[0].rearrange("e (k p) f -> p e k f", p=P)
    wu_v = w_exp_up[0].rearrange("e (k p) f -> p e k f", p=P)
    wd_v = w_exp_down[0].rearrange("e (j p) n -> p e j n", p=P)
    xs_dram = nc.dram_tensor("rows_by_expert", (XROWS, D), F32, kind="Internal").ap()
    ys_dram = nc.dram_tensor("expert_rows_out", (YROWS, D), F32, kind="Internal").ap()

    ys_more = ys_dram[NE * B:YROWS, :].rearrange("(b r) n -> r b n", r=B)
    ys_rest = ys_dram[0:NE * B, :].rearrange("(b r) n -> r b n", r=B)[B // 4:B]

    vec_list = [("ln_in_g", ln_in_g, KC), ("ln_in_b", ln_in_b, KC), ("g_attn", g_attn[0], NCH),
                ("g_ssm", g_ssm[0], NCH), ("b_glu", ssm_b_glu[0], NCH),
                ("ssm_d", ssm_d[0].rearrange("g n -> (g n)"), NCH)]
    vec_at, nvec = {}, 0
    for name, _, n in vec_list:
        vec_at[name] = nvec
        nvec += n

    with ExitStack() as ctx:
        def sb(name, shape, dt=F32):
            return ctx.enter_context(nc.sbuf_tensor(name, shape, dt))

        def sem(name):
            return ctx.enter_context(nc.semaphore(name))

        bank = ctx.enter_context(nc.psum_tensor("bank", [P, 8, 512], F32))

        xT = sb("xT", [P, KC, T])
        accT = xT
        hT = sb("hT", [P, KC, T])
        mergedT = hT
        w_ring = sb("w_ring", [P, 4, D])
        NEW = 3 * FE * D // (P * D)
        e_ring = sb("e_ring", [P, NEW, D])
        rows = sb("rows", [P, NT, D])
        DH2, FH = D // 2, FE // 2
        x_exp = rows[:, 0, 0:DH2]
        y_exp = rows[:, 1, 0:DH2]
        xT_exp = sb("xT_exp", [P, KC // 2, 2, B])
        hid = sb("hid", [P, FH])
        sig_exp = sb("sig_exp", [P, FH])
        hidT = sb("hidT", [P, FC // 2, 2, B])
        ident = sb("ident", [P, P])
        ones = sb("ones", [P, P])
        upper = sb("upper", [P, P])
        neg_half = sb("neg_half", [P, 1])
        zero_col = sb("zero_col", [P, 1])
        vecT = sb("vecT", [P, nvec])
        pT = sb("pT", [P, PLC, T])
        ple_sig = sb("ple_sig", [P, T])
        ple_tmp = sb("ple_tmp", [P, T])
        w_router = sb("w_router", [P, KC, RW])
        b_router = sb("b_router", [P, RW])
        stats = sb("stats", [P, NT, 4, 6])
        mean_var = sb("mean_var", [P, NT, 2])
        var_eps = sb("var_eps", [P, NT])
        rstd = sb("rstd", [P, NT])
        neg_mean = sb("neg_mean", [P, NT])
        idx = sb("idx", [P, 4, NT], I32)
        gate1 = sb("gate1", [P, NT])
        gate2 = sb("gate2", [P, NT])
        NTAB = NE + NOV + 2
        SHARE = 3 * D // 8
        SIZE = NTAB + NOV + 1
        tab_f = sb("tab_f", [1, SIZE + NE + 2])
        tab = sb("tab", [1, SIZE + NE + 2], I32)
        all_stored_mark = sb("all_stored_mark", [1, 1])

        used = [0]
        e_flat = e_ring[:].rearrange("p s n -> p (s n)")
        m_flat = rows[:].rearrange("p s n -> p (s n)")

        def carve(flat, shape, cursor):
            n = int(math.prod(shape))
            v = flat[:, cursor[0]:cursor[0] + n]
            cursor[0] += n
            assert cursor[0] <= flat.shape[1], cursor
            if len(shape) == 1:
                return v
            names = "abcde"[:len(shape)]
            return v.rearrange(f"p ({' '.join(names)}) -> p {' '.join(names)}",
                               **{names[i]: shape[i] for i in range(1, len(shape))})

        def early(*shape):
            return carve(e_flat, shape, used)

        attnT = early(NCH, T)
        zT = early(NCH, T)
        first_tp = [v.rearrange("p c t -> p (c t)")[:, 0:2 * JC * P].rearrange("p (r j t) -> p r j t", r=2, j=JC)
                    for v in (attnT, zT)]
        uT = early(T)
        du = early(T)
        yT = early(T)
        y2 = early(T)
        ysig = early(T)
        tmp1 = early(2, T)
        tmp2 = early(2, T)
        rot = early(2, T)
        scan = early(2, T)
        h_ssm = early(JC, 2, T)
        bn = early(2, JC, 2, GC)
        cn = early(2, 2, NS)
        bcT = early(4, P)
        bf = early(2, JC, GC)
        cf = early(2, NS)
        bt = early(4, JC, 2, GC)
        qT = early(T)
        kT = early(T)
        vT = early(T)
        ckT = early(PAST)
        ck = early(2, P)
        cv = early(2, P)
        k_nat = early(NT, P)
        v_nat = early(NT, P)
        ZW = P + TP + PAST + TS
        Z1, Z2 = P, P + TP
        zm = early(ZW)
        sig = early(ZW)
        keep = early(ZW)
        later = early(ZW + 3)
        wgt = early(ZW)
        wT = early(480)
        mask = early(P + TP)
        mask_s = early(PAST + TS)
        par_c = early(7, JC)
        d_c = early(1)
        last = early(2, 2, NJ)
        last_rows = early(4, P)
        sg = tmp2
        rms_a, rms_s = tmp1[:, 0], tmp1[:, 1]
        par = sb("par", [P, 7, NJ])
        coef = sb("coef", [P, 2, NJ, 2])
        par_b = sb("par_b", [P, 2])
        par_cg = sb("par_cg", [P, 2])
        g8 = sb("g8", [P, P // GC])
        io = sb("io", [P, NE])
        route_at, rank_at, place_at = [0], [0], [0]

        def route(*shape):
            return carve(xT_exp[:].rearrange("p k h n -> p (k h n)"), shape, route_at)

        logits = route(NT, RW)
        d5 = route(NT, NGRP + 1)
        e5 = route(NT, NGRP + 1)
        r_max = route(NT)
        r_low = route(NT)
        g_hot = route(NT, NGRP)
        el = route(NT, NE)
        pick1 = route(NT, NE)
        pick2 = route(NT, NE)
        pick = route(NT, NE)
        top1 = route(NT)
        top2 = route(NT)
        hid_flat, sig_flat = hid[:], sig_exp[:]
        counts = carve(hid_flat, (4 * NE,), rank_at)
        first_row = carve(hid_flat, (NE,), rank_at)
        more = carve(hid_flat, (NE,), rank_at)
        more_at = carve(hid_flat, (NE,), rank_at)
        jump = carve(sig_flat, (NE,), place_at)
        place = carve(sig_flat, (NT, NE), place_at)
        picked = carve(sig_flat, (NT, NE), place_at)
        sums = sb("sums", [P, 4, NT])
        w_router_flat = w_router[:].rearrange("p k n -> p (k n)")
        ov = (w_router_flat[0:1, 0:NOV * NE], w_router_flat[0:1, NOV * NE:2 * NOV * NE], route(NOV * NE)[0:1])
        sums_ov = sb("sums_ov", [1, NOV])
        in_use = sb("in_use", [1, NOV])
        gate1_diag = pT[:].rearrange("p k t -> p (k t)")[:, 0:NT * P].rearrange("p (t n) -> p t n", t=NT)
        y_fin = e_ring[:, NT:2 * NT, :]
        tb = carve(m_flat, (2, 2, JC, T), [0])
        ssmT = carve(m_flat, (NCH, T), [0])
        sq = carve(m_flat, (NCH, T), [NCH * T])
        asq = mergedT[:, NCH:KC, :]
        tp1 = carve(hT[:].rearrange("p k t -> p (k t)"), (2, JC, P), [0])
        tp2 = carve(hT[:].rearrange("p k t -> p (k t)"), (2, JC, P), [2 * JC * P])
        tail = [10 * D]
        v_rows = carve(e_flat, (P,), tail)[0:nvec, :]
        pr = carve(e_flat, (18, P), tail)[0:NJ]
        p_rows = carve(e_flat, (NT, PLC * P), tail)
        zeros_x = hT[:].rearrange("p k t -> p (k t)")[0:B, 2048:2048 + D]
        assert used[0] <= 10 * D, used

        x_landed = [sem(f"x_landed{t}") for t in range(NT)]
        small_landed = sem("small_landed")
        vec_landed = sem("vec_landed")
        p_landed = sem("p_landed")
        router_landed = sem("router_landed")
        pool_own = sem("pool_own")
        dve_own = sem("dve_own")
        ident_ready = sem("ident_ready")
        masks_ready = sem("masks_ready")
        pad_stored = sem("pad_stored")
        var_ready = sem("var_ready")
        rstd_ready = sem("rstd_ready")
        nm_ready = sem("nm_ready")
        xn_ready = sem("xn_ready")
        vecT_ready = sem("vecT_ready")
        vecT_copied = sem("vecT_copied")
        xt_ready = sem("xt_ready")
        xt_even = sem("xt_even")
        xt_odd = sem("xt_odd")
        pt_ready = sem("pt_ready")
        pt_copied = sem("pt_copied")
        pr_act_in = sem("pr_act_in")
        pr_act_out = sem("pr_act_out")
        pr_ready = sem("pr_ready")
        parT_ready = sem("parT_ready")
        par_copied = sem("par_copied")
        coef_ready = sem("coef_ready")
        w_landed = [sem(f"w_landed{s}") for s in range(4)]
        dense_done = sem("dense_done")
        bc_landed = sem("bc_landed")
        bc_ready = sem("bc_ready")
        bcT_ready = sem("bcT_ready")
        bcT_copied = sem("bcT_copied")
        table_ready = sem("table_ready")
        ck_landed = sem("ck_landed")
        cv_landed = sem("cv_landed")
        proj_copied = sem("proj_copied")
        ckT_ready = sem("ckT_ready")
        ckT_copied = sem("ckT_copied")
        du_ready = sem("du_ready")
        bu_ready = sem("bu_ready")
        bu_used = sem("bu_used")
        h_ready = sem("h_ready")
        y_part = sem("y_part")
        y_read = sem("y_read")
        last_ready = sem("last_ready")
        gelu_in = sem("gelu_in")
        gelu_sig = sem("gelu_sig")
        z_done = sem("z_done")
        z_ready = sem("z_ready")
        zm_ready = sem("zm_ready")
        sig_ready = sem("sig_ready")
        wgt_ready = sem("wgt_ready")
        wT_ready = sem("wT_ready")
        wT_copied = sem("wT_copied")
        kn_ready = sem("kn_ready")
        kn_copied = sem("kn_copied")
        vn_ready = sem("vn_ready")
        vn_copied = sem("vn_copied")
        k_stored = sem("k_stored")
        v_stored = sem("v_stored")
        a_ready = sem("a_ready")
        a_copied = sem("a_copied")
        lastT_ready = sem("lastT_ready")
        last_copied = sem("last_copied")
        last_stored = sem("last_stored")
        asq_ready = sem("asq_ready")
        ass_ready = sem("ass_ready")
        glu_sig = sem("glu_sig")
        s_ready = sem("s_ready")
        ssq_ready = sem("ssq_ready")
        sss_ready = sem("sss_ready")
        ms_ready = sem("ms_ready")
        rms_root = sem("rms_root")
        rms_ready = sem("rms_ready")
        merged_a = sem("merged_a")
        merged_s = sem("merged_s")
        res_ready = sem("res_ready")
        nat_ready = sem("nat_ready")
        var1_ready = sem("var1_ready")
        rstd1_ready = sem("rstd1_ready")
        nm1_ready = sem("nm1_ready")
        xh_ready = sem("xh_ready")
        gb1_landed = sem("gb1_landed")
        hg_ready = sem("hg_ready")
        h_rows_pool = sem("h_rows_pool")
        h_rows_dve = sem("h_rows_dve")
        hT_ready = sem("hT_ready")
        hT_copied = sem("hT_copied")
        logits_ready = sem("logits_ready")
        exp_in = sem("exp_in")
        exp_out = sem("exp_out")
        pick_ready = sem("pick_ready")
        rank_ready = sem("rank_ready")
        idx_ready = sem("idx_ready")
        tab_ready = sem("tab_ready")
        rows_sorted = sem("rows_sorted")
        ew_landed = [sem(f"ew_landed{s}") for s in range(NEW)]
        ew_used = sem("ew_used")
        xe_landed = sem("xe_landed")
        xeT_ready = sem("xeT_ready")
        xeT_act = sem("xeT_act")
        xeT_dve = sem("xeT_dve")
        gsig_ready = sem("gsig_ready")
        gmul_ready = sem("gmul_ready")
        hid_ready = sem("hid_ready")
        hidT_ready = sem("hidT_ready")
        hidT_copied = sem("hidT_copied")
        ye_act = sem("ye_act")
        ye_dve = sem("ye_dve")
        ye_stored = sem("ye_stored")
        plg_sig = sem("plg_sig")
        ple_mul = sem("ple_mul")
        ple_done = sem("ple_done")
        all_stored = sem("all_stored")
        gb2_landed = sem("gb2_landed")
        y1_gathered = [sem(f"y1_gathered{t}") for t in range(NT)]
        y2_gathered = [sem(f"y2_gathered{t}") for t in range(NT)]
        diag_ready = sem("diag_ready")
        fin_nat = sem("fin_nat")
        fin_var = sem("fin_var")
        fin_sum = sem("fin_sum")
        fin_rstd = sem("fin_rstd")
        fin_nm = sem("fin_nm")
        fin_xh = sem("fin_xh")
        fin_g = sem("fin_g")
        fin_b = sem("fin_b")
        fin_b_dve = sem("fin_b_dve")
        y_stored = sem("y_stored")

        block = ctx.enter_context(nc.Block())

        N_GLU = 4 * NCH
        N_OUT = N_GLU + NCH
        N_PLE = N_OUT + KC
        EARLY_GATE, EARLY_PROJ = (1, 2), (3, 4)
        EARLY_PLE = 2
        PLE_PAIRS = KC - EARLY_PLE
        PAD_STORES = 16 * (1 + NOV // 3 + NCH)
        LAST_C = NCH

        def further_blocks(eng, body):
            count = eng.value_load(tab[0:1, NTAB + NOV:NTAB + NOV + 1], min_val=0, max_val=NOV)
            with eng.If(count > 0):
                with eng.Fori(0, NOV) as i:
                    with eng.If(count > i):
                        body(i)
            return count

        def hT_bank(t, q):
            return bank[:, 4 + q, :] if t == 0 else bank[:, q, :] if t == 1 else bank[:, 5, 4 * q * TS:4 * (q + 1) * TS]

        def table(eng, own, c, cb, tp1, tp2):
            w = tb[:, cb]
            own(eng.tensor_tensor(w[:, :, :, 0], par[:, 1:3, ds(c * JC, JC)],
                                  ones[:, 0:2 * JC].rearrange("p (r j) -> p r j", r=2), ALU.mult))
            own.wait()
            k = 1
            while k < TP:
                s4 = [P, 2, JC, k]
                own(eng.tensor_tensor(tp1[:, :, :, 0:k], w[:, :, :, 0:k],
                                      w[:, 0:1, :, k - 1:k].to_broadcast(s4), ALU.mult))
                own(eng.tensor_tensor(tp2[:, :, :, 0:k], w[:, :, :, 0:k],
                                      w[:, 1:2, :, k - 1:k].to_broadcast(s4), ALU.mult))
                own.wait()
                own(eng.tensor_tensor(w[:, 0, :, k:2 * k], tp1[:, 0, :, 0:k], tp2[:, 1, :, 0:k], ALU.subtract))
                own(eng.tensor_tensor(w[:, 1, :, k:2 * k], tp1[:, 1, :, 0:k], tp2[:, 0, :, 0:k], ALU.add))
                own.wait()
                k *= 2
            return eng.tensor_tensor(w[:, :, :, TP:T], w[:, :, :, 0:TS],
                                     ones[:, 0:1].unsqueeze(1).unsqueeze(1).to_broadcast([P, 2, JC, TS]), ALU.mult)

        @block.sync
        def _(sp):
            def x_load(t):
                sp.dma_start(rows[0:TT[t][1], t, :], x_src[t]).then_inc(x_landed[t], 16)

            x_load(IN_ORDER[0])
            x_load(IN_ORDER[1])
            for f, src in enumerate(rows_v):
                sp.dma_start(pr[:, f, :], src).then_inc(small_landed, 16)
            with nc.allow_non_contiguous_dma(reason="64 values"):
                sp.dma_start(pr[:, 4, 0:2], step_v).then_inc(small_landed, 16)
            x_load(IN_ORDER[2])
            for name, src, n in vec_list:
                a = vec_at[name]
                sp.dma_start(v_rows[a:a + n, :], src.rearrange("(k p) -> k p", p=P)).then_inc(vec_landed, 16)

            def settled():
                sp.wait_ge(x_landed[IN_ORDER[0]], 16)

            def w_load(slot, wait, src, width=P):
                if wait is not None:
                    sp.wait_ge(dense_done, wait)
                    settled()
                sp.dma_start(w_ring[:, slot, 0:src.shape[1] * width].rearrange("p (k n) -> p k n", n=width),
                             src).then_inc(w_landed[slot], 16)

            def chunk(c, first):
                if not first:
                    sp.wait_ge(bc_ready, c)
                    settled()
                for r in range(2):
                    sp.dma_start(bf[:, r], b_v[r][:, c]).then_inc(bc_landed, 16)
                    sp.dma_start(cf[:, r], c_v[r][:, c]).then_inc(bc_landed, 16)
                for s, part in enumerate((3, 0, 1, 2)):
                    if s == 1:
                        if not first:
                            settled()
                            sp.wait_ge(ckT_ready, c)
                        sp.dma_start(ck, ck_v[:, :, c, :]).then_inc(ck_landed, 16)
                    w_load(s, None if first else c * 4 + (s - 3),
                           w_in_v[:, :, ds(part * W + c * P, P)])

            chunk(0, True)
            for t, (_, m) in enumerate(TT):
                sp.dma_start(p_rows[0:m, t, :], p_src[t]).then_inc(p_landed, 16)
            sp.dma_start(w_router[:, :, 0:NGRP], w_router_group[0].rearrange("(k p) n -> p k n", p=P)).then_inc(router_landed, 16)
            sp.dma_start(w_router[:, :, NGRP:RW], w_router_expert[0].rearrange("(k p) n -> p k n", p=P)).then_inc(router_landed, 16)
            sp.dma_start(b_router[:, 0:NGRP], b_router_group[0].partition_broadcast(P)).then_inc(router_landed, 16)
            sp.dma_start(b_router[:, NGRP:RW], b_router_expert[0].partition_broadcast(P)).then_inc(router_landed, 16)
            with sp.Fori(1, NCH) as c:
                chunk(c, False)
            for s in range(4):
                w_load(s, N_GLU + s - 3, w_glu_v[:, :, 2 * s * P:2 * (s + 1) * P], 2 * P)
            for s in range(4):
                w_load(s, N_GLU + 2 * s + 2, w_out_v[:, :, s * P:(s + 1) * P])

            def expert_piece(b, e, s, first):
                if not first:
                    sp.wait_ge(ew_used, b * NEW + (s + 1 - NEW))
                    settled()
                if s < 8:
                    src = (wg_v, wu_v)[s % 2][:, ds(e, 1), 4 * (s // 2):4 * (s // 2) + 4, :]
                    dst = e_ring[:, s, :].rearrange("p (a k f) -> p a k f", a=1, k=4)
                else:
                    src = wd_v[:, ds(e, 1), s - 8, :]
                    dst = e_ring[:, s:s + 1, :]
                sp.dma_start(dst, src).then_inc(ew_landed[s], 16)

            def expert_load(b, e):
                for s in range(NEW):
                    expert_piece(b, e, s, False)

            sp.wait_ge(merged_s, NCH)
            sp.wait_ge(last_stored, 64)
            sp.wait_ge(pt_copied, PLC)
            for m in range(4, KC):
                w_load(m % 4, N_OUT + m - 3, w_out_v[:, :, m * P:(m + 1) * P])
                expert_piece(0, 0, m - 4, True)
            sp.wait_ge(dense_done, N_PLE)
            sp.dma_start(w_ring[:, 2, :], ln1_g[0].partition_broadcast(P)).then_inc(gb1_landed, 16)
            sp.dma_start(w_ring[:, 3, :], ln1_b[0].partition_broadcast(P)).then_inc(gb1_landed, 16)

            def ple_load(c, slot, at, gate_wait, proj_wait):
                if gate_wait is not None:
                    sp.wait_ge(dense_done, gate_wait)
                    settled()
                sp.dma_start(w_ring[:, slot, :].rearrange("p (k n) -> p k n", n=P), w_plg_v[:, :, ds(c * P, P)]).then_inc(w_landed[slot], 16)
                if proj_wait is not None:
                    sp.wait_ge(dense_done, proj_wait)
                    settled()
                sp.dma_start(w_ring[:, 1, at:at + PLC * P].rearrange("p (k n) -> p k n", n=P), w_plp_v[:, :, ds(c * P, P)]).then_inc(w_landed[1], 16)

            ple_load(0, 0, 0, None, None)
            sp.wait_ge(h_rows_pool, NT)
            sp.wait_ge(h_rows_dve, NT)
            for c in range(1, EARLY_PLE):
                ple_load(c, c + 1, c * PLC * P, None, None)
            sp.dma_start(w_ring[:, 3, :], ln2_b[0].partition_broadcast(P)).then_inc(gb2_landed, 16)
            sp.wait_ge(dense_done, N_PLE + EARLY_GATE[1])
            sp.wait_ge(xe_landed, 32)
            sp.dma_start(w_ring[:, 2, :], ln2_g[0].partition_broadcast(P)).then_inc(gb2_landed, 16)
            ple_load(EARLY_PLE, 0, 0, N_PLE + 2 * EARLY_PLE - 1, N_PLE + 2 * EARLY_PLE)
            expert_load(1, 1)
            with sp.Fori(1, PLE_PAIRS) as i:
                ple_load(i + EARLY_PLE, 0, 0, i * 2 + (N_PLE + 2 * EARLY_PLE - 1), i * 2 + (N_PLE + 2 * EARLY_PLE))
                expert_load(i * 2, i * 2)
                expert_load(i * 2 + 1, i * 2 + 1)
            with sp.Fori(2 * PLE_PAIRS, NE) as b:
                expert_load(b, b)
            sp.wait_ge(tab_ready, 1)

            def further(i):
                e = sp.value_load(tab[0:1, ds(i + NTAB, 1)], min_val=0, max_val=NE - 1)
                expert_load(i + NE, e)

            further_blocks(sp, further)
            for t, (_, m) in enumerate(TT):
                sp.wait_ge(fin_b, t + 1)
                if t:
                    sp.wait_ge(fin_b_dve, t)
                sp.dma_start(y_dst[t], y_fin[0:m, t, :]).then_inc(y_stored, 16)
            sp.wait_ge(y_stored, 16 * NT)

        @block.gpsimd
        def _(pool):
            own = OwnOrder(pool, pool_own)
            own(pool.memset(ident[:], 0.0))
            own(pool.memset(ones[:], 1.0))
            own(pool.memset(mask, 0.0))
            own(pool.memset(mask_s, 0.0))
            own(pool.memset(neg_half[:], -0.5))
            own.wait()
            pool.affine_select(out=ident[:], in_=ident[:], compare_op=ALU.not_equal, fill=1.0, base=0,
                               pattern=[[-1, P]], channel_multiplier=1).then_inc(ident_ready, 1)
            own(pool.affine_select(out=upper[:], in_=ones[:], compare_op=ALU.is_gt, fill=0.0, base=0,
                                   pattern=[[1, P]], channel_multiplier=-1))
            for view, m in ((mask[:, 0:P], P), (mask[:, P + P:P + 2 * P], P), (mask_s[0:TS, PAST:PAST + TS], TS)):
                own(pool.affine_select(out=view, in_=view, compare_op=ALU.is_gt, fill=NEG, base=0,
                                       pattern=[[-1, m]], channel_multiplier=1))
            own(pool.affine_select(out=par_b[:, 0:1], in_=ones[:, 0:1], compare_op=ALU.is_ge, fill=0.0, base=NS - 1,
                                   pattern=[[0, 1]], channel_multiplier=-1))
            own(pool.affine_select(out=par_b[:, 1:2], in_=ones[:, 0:1], compare_op=ALU.is_ge, fill=0.0, base=-NS,
                                   pattern=[[0, 1]], channel_multiplier=1))
            own(pool.affine_select(out=g8[:], in_=ones[:, 0:P // GC], compare_op=ALU.is_ge, fill=0.0, base=0,
                                   pattern=[[-GC, P // GC]], channel_multiplier=1))
            own.wait()
            own(pool.affine_select(out=g8[:], in_=g8[:], compare_op=ALU.is_ge, fill=0.0, base=GC - 1,
                                   pattern=[[GC, P // GC]], channel_multiplier=-1))
            own.wait()
            g8v = g8[:].rearrange("p (i a) -> p a i", a=2)
            folded = tmp1[:, 0, 0:4].rearrange("p (a i) -> p a i", a=2)
            own(pool.tensor_tensor(folded, g8v[:, :, 0:2], g8v[:, :, 2:4], ALU.add))
            own.wait()
            own(pool.tensor_tensor(par_cg[:], folded[:, :, 0], folded[:, :, 1], ALU.add))
            own.wait()
            pool.iota(io[:], [[1, NE]], base=0, channel_multiplier=0,
                      allow_small_or_imprecise_dtypes=True).then_inc(masks_ready, 1)
            for n, t in enumerate(IN_ORDER):
                m = TT[t][1]
                pool.wait_ge(var_ready, n + 1)
                pool.tensor_tensor(rstd[0:m, t:t + 1], var_eps[0:m, t:t + 1], neg_half[0:m, :], ALU.pow).then_inc(rstd_ready, 1)
            own(pool.memset(zeros_x, 0.0))

            pool.wait_ge(coef_ready, 1)
            pool.wait_ge(xt_ready, KC)

            def clear_rest(c):
                n = NE // NCH
                pool.dma_start(ys_rest[:, ds(c * n, n), :], zeros_x[B // 4:B, :].unsqueeze(1).to_broadcast([B - B // 4, n, D])).then_inc(pad_stored, 16)

            def chunk(c, cb, first, early_chunk=False):
                pool.wait_ge(bc_landed, c * 64 + 64)
                if not first:
                    pool.wait_ge(bcT_ready, c)
                pool.wait_ge(coef_ready, 1)
                shp = [P, JC, 2, GC]
                bre, bim = (bf[:, r].unsqueeze(2).to_broadcast(shp) for r in range(2))
                cre, cim = (coef[:, r, ds(c * JC, JC), :].unsqueeze(3).to_broadcast(shp) for r in range(2))
                own(pool.tensor_tensor(bt[:, 0], bre, cre, ALU.mult))
                own(pool.tensor_tensor(bt[:, 1], bim, cim, ALU.mult))
                own(pool.tensor_tensor(bt[:, 2], bre, cim, ALU.mult))
                own(pool.tensor_tensor(bt[:, 3], bim, cre, ALU.mult))
                for a in range(2):
                    own(pool.tensor_scalar(cn[:, 0, a, :], cf[:, 0, :], par_cg[:, a:a + 1], 1.0, ALU.mult, ALU.mult))
                    own(pool.tensor_scalar(cn[:, 1, a, :], cf[:, 1, :], par_cg[:, a:a + 1], -1.0, ALU.mult, ALU.mult))
                own.wait()
                own(pool.tensor_tensor(bn[:, 0], bt[:, 0], bt[:, 1], ALU.subtract))
                own.wait()
                pool.tensor_tensor(bn[:, 1], bt[:, 2], bt[:, 3], ALU.add).then_inc(bc_ready, 1)
                if early_chunk:
                    return
                pool.wait_ge(last_ready, (c - 1) * JC)
                pool.wait_ge(coef_ready, 1)
                table(pool, own, c, cb, tp1, tp2).then_inc(table_ready, 1)
                clear_rest(c)

            chunk(0, 0, True, True)
            table(pool, own, 1, 1, tp1, tp2).then_inc(table_ready, 1)
            chunk(1, 1, False, True)
            pool.dma_start(xs_dram[2 * T:XROWS, :], zeros_x).then_inc(pad_stored, 16)
            for i in range(0, NOV, 3):
                pool.dma_start(ys_more[:, i:i + 3, :], zeros_x.unsqueeze(1).to_broadcast([B, 3, D])).then_inc(pad_stored, 16)
            clear_rest(0)
            clear_rest(1)
            base = own.base + own.n
            with pool.Fori(1, NCH // 2) as i:
                own.enter((i - 1) * POOL_PER_PAIR + base)
                chunk(i * 2, 0, False)
                chunk(i * 2 + 1, 1, False)
                assert own.n == POOL_PER_PAIR, own.n
            own.enter(base + (NCH // 2 - 1) * POOL_PER_PAIR)
            for t, (_, m) in enumerate(TT):
                pool.wait_ge(var1_ready, t + 1)
                pool.tensor_tensor(rstd[0:m, t:t + 1], var_eps[0:m, t:t + 1], neg_half[0:m, :], ALU.pow).then_inc(rstd1_ready, 1)
            for t, (_, m) in enumerate(TT):
                pool.wait_ge(hg_ready, t + 1)
                pool.tensor_tensor(rows[0:m, t, 0:SHARE], rows[0:m, t, 0:SHARE], w_ring[0:m, 3, 0:SHARE], ALU.add).then_inc(h_rows_pool, 1)
            pool.wait_ge(idx_ready, 1)
            pool.wait_ge(h_rows_pool, NT)
            pool.wait_ge(h_rows_dve, NT)
            for k in range(2):
                for t, (_, m) in enumerate(TT):
                    pool.indirect_dma_start(xs_dram[:, :], bass.IndirectOffsetOnAxis(ap=idx[0:m, k, t:t + 1], axis=0),
                                            rows[0:m, t, :], None).then_inc(rows_sorted, 16)
            pool.wait_ge(all_stored, 1)
            pool.wait_ge(idx_ready, 2)
            for t, (_, m) in enumerate(TT):
                for k in range(2):
                    pool.indirect_dma_start(e_ring[0:m, k * NT + t, :], None, ys_dram[:, :],
                                            bass.IndirectOffsetOnAxis(ap=idx[0:m, 2 + k, t:t + 1], axis=0)).then_inc((y1_gathered, y2_gathered)[k][t], 16)
            def fin_root(t, m):
                pool.wait_ge(fin_var, t + 1)
                pool.tensor_tensor(rstd[0:m, t:t + 1], var_eps[0:m, t:t + 1], neg_half[0:m, :], ALU.pow).then_inc(fin_rstd, 1)

            def fin_gain(t, m):
                pool.wait_ge(fin_xh, t + 1)
                pool.tensor_tensor(y_fin[0:m, t, :], y_fin[0:m, t, :], w_ring[0:m, 2, :], ALU.mult).then_inc(fin_g, 1)

            def fin_bias(t, m):
                pool.wait_ge(fin_g, t + 1)
                n = SHARE if t else D
                pool.tensor_tensor(y_fin[0:m, t, 0:n], y_fin[0:m, t, 0:n], w_ring[0:m, 3, 0:n], ALU.add).then_inc(fin_b, 1)

            pool.wait_ge(gb2_landed, 32)
            fin_root(0, P)
            fin_gain(0, P)
            fin_root(1, P)
            fin_bias(0, P)
            fin_root(2, TS)
            fin_bias(1, P)
            fin_bias(2, TS)

        @block.scalar
        def _(act):
            def copy(out, in_):
                return act.activation(out, in_, ACT.Copy)

            act.wait_ge(small_landed, 80)
            act.activation(pr[:, 4, 2:4], pr[:, 4, 0:2], ACT.Exp).then_inc(pr_act_out, 1)
            act.wait_ge(pr_act_in, 1)
            act.activation(pr[:, 8, :], pr[:, 5, :], ACT.Exp).then_inc(pr_act_out, 1)
            act.activation(pr[:, 9:11, :], pr[:, 11:13, :], ACT.Sin).then_inc(pr_act_out, 1)
            act.wait_ge(vecT_ready, 1)
            copy(vecT[:], bank[:, 7, 0:nvec]).then_inc(vecT_copied, 1)
            act.wait_ge(vecT_copied, 1)
            for n, t in enumerate(IN_ORDER):
                m = TT[t][1]
                act.wait_ge(nm_ready, n + 1)
                act.activation(rows[0:m, t, :], rows[0:m, t, :], ACT.Identity, scale=rstd[0:m, t:t + 1],
                               bias=neg_mean[0:m, t:t + 1]).then_inc(xn_ready, 1)
            for k in range(0, KC, 2):
                if k == KC // 2 + 2:
                    act.wait_ge(parT_ready, 1)
                    copy(par[:].rearrange("p f j -> p (f j)"), bank[:, 5, 0:7 * NJ]).then_inc(par_copied, 1)
                act.wait_ge(xt_ready, k + 1)
                a, b = vec_at["ln_in_g"] + k, vec_at["ln_in_b"] + k
                act.activation(xT[:, k, :], bank[:, k % 4, 0:T], ACT.Identity, scale=vecT[:, a:a + 1],
                               bias=vecT[:, b:b + 1]).then_inc(xt_even, 1)

            def gate(m):
                if m < NCH:
                    act.wait_ge(dense_done, N_GLU + m + 1)
                    if m >= 2:
                        act.wait_ge(s_ready, m - 1)
                    a = vec_at["b_glu"] + m
                    act.activation(sg[:, m % 2], bank[:, m % 4, 0:T], ACT.Sigmoid, bias=vecT[:, a:a + 1]).then_inc(glu_sig, 1)
                if m:
                    act.wait_ge(s_ready, m)
                    act.activation(sq[:, m - 1], ssmT[:, m - 1], ACT.Square).then_inc(ssq_ready, 1)

            def chunk(c, cur, prev, first):
                if cur:
                    act.wait_ge(dense_done, c * 4 + 1)
                    if prev:
                        act.wait_ge(du_ready, c)
                    copy(uT, bank[:, 0, 0:T]).then_inc(proj_copied, 1)
                    act.wait_ge(bcT_ready, c + 1)
                    copy(bcT.rearrange("p f n -> p (f n)"), bank[:, 7, 0:4 * P]).then_inc(bcT_copied, 1)
                if prev:
                    act.wait_ge(zm_ready, c)
                    if not first:
                        act.wait_ge(wgt_ready, c - 1)
                    act.activation(sig[:, 0:Z2], zm[:, 0:Z2], ACT.Sigmoid)
                    act.activation(sig[0:TS, Z2:ZW], zm[0:TS, Z2:ZW], ACT.Sigmoid)
                    act.activation(keep[:, 0:Z2], zm[:, 0:Z2], ACT.Sigmoid, scale=-1.0)
                    act.activation(keep[0:TS, Z2:ZW], zm[0:TS, Z2:ZW], ACT.Sigmoid, scale=-1.0).then_inc(sig_ready, 1)
                    act.wait_ge(kn_ready, c)
                    if not first:
                        act.wait_ge(k_stored, (c - 1) * 32)
                    copy(k_nat[:, 0:2, :], bank[:, 7, 0:2 * P].rearrange("p (t n) -> p t n", t=2)).then_inc(kn_copied, 1)
                    copy(k_nat[0:TS, 2, :], bank[0:TS, 7, 2 * P:3 * P]).then_inc(kn_copied, 1)
                    act.wait_ge(kn_copied, c * 2)
                    act.dma_start(kp_v[:, :, c - 1, :], k_nat[:, 0:2, :]).then_inc(k_stored, 16)
                    act.dma_start(k_sample[0, 0, :, c - 1, :], k_nat[0:TS, 2, :]).then_inc(k_stored, 16)
                    act.wait_ge(gelu_in, c)
                    if not first:
                        act.wait_ge(z_done, c - 1)
                    act.activation(ysig, y2, ACT.Sigmoid, scale=2.0 * math.sqrt(2.0 / math.pi) * 0.044715).then_inc(gelu_sig, 1)
                if cur:
                    act.wait_ge(dense_done, c * 4 + 2)
                    copy(qT, bank[:, 1, 0:T]).then_inc(proj_copied, 1)
                    act.wait_ge(ckT_ready, c + 1)
                    copy(ckT, bank[:, 7, 0:PAST]).then_inc(ckT_copied, 1)
                    act.wait_ge(dense_done, c * 4 + 3)
                    copy(kT, bank[:, 0, 0:T]).then_inc(proj_copied, 1)
                if prev:
                    act.wait_ge(vn_ready, c)
                    if not first:
                        act.wait_ge(v_stored, (c - 1) * 32)
                    copy(v_nat[:, 0:2, :], bank[:, 7, 0:2 * P].rearrange("p (t n) -> p t n", t=2)).then_inc(vn_copied, 1)
                    copy(v_nat[0:TS, 2, :], bank[0:TS, 7, 2 * P:3 * P]).then_inc(vn_copied, 1)
                    act.wait_ge(wT_ready, c)
                    copy(wT[:, 0:448], bank[:, 5, 0:448]).then_inc(wT_copied, 1)
                    copy(wT[0:TS, 448:480], bank[0:TS, 5, 448:480]).then_inc(wT_copied, 1)
                    act.wait_ge(vn_copied, c * 2)
                    act.dma_start(vp_v[:, :, c - 1, :], v_nat[:, 0:2, :]).then_inc(v_stored, 16)
                    act.dma_start(v_sample[0, 0, :, c - 1, :], v_nat[0:TS, 2, :]).then_inc(v_stored, 16)
                if cur:
                    act.wait_ge(dense_done, c * 4 + 4)
                    copy(vT, bank[:, 1, 0:T]).then_inc(proj_copied, 1)
                if not cur:
                    act.wait_ge(last_ready, NJ)
                    for m in range(4):
                        gate(m)
                if prev:
                    act.wait_ge(a_ready, c)
                    copy(attnT[:, ds(c - 1, 1), :].rearrange("p a t -> p (a t)"), bank[:, 6, 0:T]).then_inc(a_copied, 1)
                if cur:
                    act.dma_start(cv, cv_v[:, :, c, :]).then_inc(cv_landed, 16)

            chunk(0, True, False, True)
            chunk(1, True, True, True)
            with act.Fori(2, NCH) as c:
                chunk(c, True, True, False)
            chunk(LAST_C, False, True, False)

            act.wait_ge(a_copied, NCH)
            act.wait_ge(table_ready, NCH - 1)
            act.wait_ge(pad_stored, PAD_STORES)
            act.activation(asq, attnT, ACT.Square).then_inc(asq_ready, 1)
            gate(4)
            gate(5)
            act.wait_ge(lastT_ready, 1)
            copy(last_rows[0:NJ], bank[0:NJ, 6, 0:4 * P].rearrange("p (f n) -> p f n", f=4)).then_inc(last_copied, 1)
            act.wait_ge(last_copied, 1)
            for f in range(4):
                act.dma_start(last_v[f], last_rows[0:NJ, f, :]).then_inc(last_stored, 16)
            act.wait_ge(ms_ready, 1)
            act.activation(rms_a, rms_a, ACT.Sqrt).then_inc(rms_root, 1)
            for m in range(6, NCH + 1):
                gate(m)
            act.wait_ge(ms_ready, 2)
            act.activation(rms_s, rms_s, ACT.Sqrt).then_inc(rms_root, 1)
            for k in range(PLC):
                act.wait_ge(pt_ready, k + 1)
                copy(pT[:, k, :], bank[:, 4 if k else 6, 0:T]).then_inc(pt_copied, 1)
            for t, (_, m) in enumerate(TT):
                act.wait_ge(nm1_ready, t + 1)
                b0 = 4 * (t % 2)
                act.activation(rows[0:m, t, :], bank[0:m, b0:b0 + 4, :].rearrange("p b n -> p (b n)"), ACT.Identity,
                               scale=rstd[0:m, t:t + 1], bias=neg_mean[0:m, t:t + 1]).then_inc(xh_ready, 1)
            for t in range(2):
                for q in range(4):
                    act.wait_ge(hT_ready, 4 * t + q + 1)
                    copy(hT[:, 4 * q:4 * q + 4, t * P:(t + 1) * P], hT_bank(t, q).rearrange("p (k n) -> p k n", k=4)).then_inc(hT_copied, 1)
            act.wait_ge(hT_ready, 9)
            copy(hT[:, :, TP:T], bank[:, 5, :].rearrange("p (k n) -> p k n", k=KC)).then_inc(hT_copied, 1)
            act.wait_ge(exp_in, 1)
            act.activation(e5, d5, ACT.Exp).then_inc(exp_out, 1)

            def by_size(b, further, move):
                if further:
                    move(B)
                    return
                size = act.value_load(tab[0:1, ds(b + SIZE, 1)], min_val=0, max_val=2)
                with act.If(size > 1):
                    move(B)
                with act.Else():
                    with act.If(size > 0):
                        move(B // 2)
                    with act.Else():
                        move(B // 4)

            def x_load(b, further=False):
                row = act.value_load(tab[0:1, ds(b, 1)], min_val=0, max_val=2 * T)

                def move(n):
                    for h in range(2):
                        act.dma_start(x_exp[h * B:h * B + n, :], xs_dram[ds(row, n), h * DH2:(h + 1) * DH2]).then_inc(xe_landed, 16)
                by_size(b, further, move)

            def y_store(b, further):
                def move(n):
                    for h in range(2):
                        act.dma_start(ys_dram[ds(b * B, n), h * DH2:(h + 1) * DH2], y_exp[h * B:h * B + n, :]).then_inc(ye_stored, 16)
                by_size(b, further, move)

            def x_copy(b):
                act.wait_ge(xeT_ready, b + 1)
                copy(xT_exp[:, 0:4].rearrange("p k h n -> p (k h n)"), bank[:, 1, :]).then_inc(xeT_act, 1)

            def expert(b, first, middle=None, further=False):
                act.wait_ge(ew_used, b * NEW + 8)
                act.activation(sig_exp[:], bank[:, 0, 0:FH], ACT.Sigmoid).then_inc(gsig_ready, 1)
                x_copy(b + 1)
                x_load(b + 2, further)
                if middle is not None:
                    middle()
                act.wait_ge(ew_used, b * NEW + NEW)
                if not first:
                    act.wait_ge(ye_stored, b * 32)
                copy(y_exp[:, 0:512], bank[:, 3, :]).then_inc(ye_act, 1)
                act.wait_ge(ye_act, b + 1)
                act.wait_ge(ye_dve, b + 1)
                y_store(b, further)

            def ple_gate(c, bank_no=7, done=None):
                act.wait_ge(dense_done, done or c * 2 + (N_PLE + 1))
                if not (done and c == 0):
                    act.wait_ge(ple_mul, c)
                act.activation(ple_sig[:], bank[:, bank_no, 0:T], ACT.Sigmoid).then_inc(plg_sig, 1)

            def pair(i, first):
                expert(i * 2, first, lambda: ple_gate(i + EARLY_PLE))
                expert(i * 2 + 1, False)

            for c in range(EARLY_PLE):
                ple_gate(c, 7 - c, N_PLE + EARLY_GATE[c])
            act.wait_ge(tab_ready, 1)
            act.wait_ge(rows_sorted, 16 * 2 * NT)
            x_load(0)
            x_copy(0)
            x_load(1)
            pair(0, True)
            with act.Fori(1, PLE_PAIRS) as i:
                pair(i, False)
            with act.Fori(2 * PLE_PAIRS, NE) as b:
                expert(b, False)
            count = further_blocks(act, lambda i: expert(i + NE, False, further=True))
            act.wait_ge(ye_stored, count * 32 + NE * 32)
            act.wait_ge(xe_landed, count * 32 + (NE + 2) * 32)
            copy(all_stored_mark[:], zero_col[0:1, 0:1]).then_inc(all_stored, 1)
            for t, (_, m) in enumerate(TT):
                act.wait_ge(fin_nm, t + 1)
                act.activation(y_fin[0:m, t, :], y_fin[0:m, t, :], ACT.Identity,
                               scale=rstd[0:m, t:t + 1], bias=neg_mean[0:m, t:t + 1]).then_inc(fin_xh, 1)

        @block.tensor
        def _(pe):
            def dense(out, weights, moving, n):
                for k in range(n):
                    last_mm = pe.matmul(out, weights(k), moving[:, k, :], start=(k == 0), stop=(k == n - 1))
                return last_mm

            pe.wait_ge(ident_ready, 1)
            pe.wait_ge(vec_landed, 16 * len(vec_list))
            pe.transpose(bank[:, 7, 0:nvec], v_rows, ident[0:nvec, 0:nvec]).then_inc(vecT_ready, 1)
            pe.wait_ge(xn_ready, NT)
            for k in range(KC):
                if k >= 4:
                    pe.wait_ge(xt_odd if k % 2 else xt_even, (k - 4) // 2 + 1)
                for t, (t0, m) in enumerate(TT):
                    mm = pe.transpose(bank[:, k % 4, t0:t0 + m], rows[0:m, t, k * P:(k + 1) * P], ident[0:m, 0:m])
                mm.then_inc(xt_ready, 1)
                if k == KC // 2 - 1:
                    pe.wait_ge(pr_ready, 1)
                    for i, f in enumerate((8, 9, 10, 16, 17, 2, 3)):
                        mm = pe.transpose(bank[:, 5, i * NJ:(i + 1) * NJ], pr[:, f, :], ident[0:NJ, 0:NJ])
                    mm.then_inc(parT_ready, 1)
            pe.wait_ge(xt_even, KC // 2)
            pe.wait_ge(xt_odd, KC // 2)
            pe.wait_ge(par_copied, 1)

            def proj(c, s, first):
                pe.wait_ge(w_landed[s], c * 16 + 16)
                if not (first and s < 2):
                    pe.wait_ge(proj_copied, c * 4 + s - 1)
                w = w_ring[:, s, :].rearrange("p (k n) -> p k n", n=P)
                dense(bank[:, s % 2, 0:T], lambda k: w[:, k, :], xT, KC).then_inc(dense_done, 1)

            def bu(c, i, first):
                if not (first and i == 0):
                    pe.wait_ge(bu_used, c * JC + i)
                for r in range(2):
                    mm = pe.matmul(bank[:, 2 + r, 0:T], bcT[32 * i:32 * i + 32, r, :], uT[32 * i:32 * i + 32, :], start=True, stop=True)
                mm.then_inc(bu_ready, 1)

            def y_out(c, h):
                pe.wait_ge(h_ready, c * JC + 2 * h + 2)
                for r in range(2):
                    for i in (2 * h, 2 * h + 1):
                        mm = pe.matmul(bank[32 * i:32 * i + 32, 4, 0:T], bcT[:, 2 + r, 32 * i:32 * i + 32], h_ssm[:, i, r, :],
                                       start=(r == 0), stop=(r == 1))
                mm.then_inc(y_part, 1)

            def chunk(c, cur, prev, first):
                if cur:
                    proj(c, 0, not prev)
                if not cur:
                    glu_start(0)
                    glu_start(1)
                if prev:
                    y_out(c - 1, 1)
                if cur:
                    pe.wait_ge(bc_ready, c + 1)
                    if prev and not first:
                        pe.wait_ge(vn_copied, (c - 1) * 2)
                    if prev:
                        pe.wait_ge(ckT_copied, c)
                    for r in range(2):
                        pe.transpose(bank[:, 7, r * P:(r + 1) * P], bn[:, r].rearrange("p j a n -> p (j a n)"), ident[:])
                    for r in range(2):
                        mm = pe.transpose(bank[:, 7, (2 + r) * P:(3 + r) * P], cn[:, r].rearrange("p a n -> p (a n)"), ident[:])
                    mm.then_inc(bcT_ready, 1)
                if prev:
                    pe.wait_ge(proj_copied, c * 4)
                    if not first:
                        pe.wait_ge(wT_copied, (c - 1) * 2)
                        pe.wait_ge(a_copied, c - 1)
                    pe.wait_ge(ckT_copied, c)
                    pe.matmul(bank[:, 5, 0:Z1], qT[:, 0:P], kT[:, 0:P], start=True, stop=True)
                    pe.matmul(bank[:, 5, Z1:Z2], qT[:, P:TP], kT[:, 0:TP], start=True, stop=True)
                    pe.matmul(bank[0:TS, 6, 0:PAST], qT[:, TP:T], ckT, start=True, stop=True)
                    pe.matmul(bank[0:TS, 6, PAST:PAST + TS], qT[:, TP:T], kT[:, TP:T], start=True, stop=True).then_inc(z_ready, 1)
                if cur:
                    pe.wait_ge(proj_copied, c * 4 + 1)
                    pe.wait_ge(bcT_copied, c + 1)
                    bu(c, 0, not prev)
                if prev:
                    if not cur:
                        pe.wait_ge(ckT_copied, c)
                    for t, (t0, m) in enumerate(TT):
                        mm = pe.transpose(bank[0:m, 7, t * P:(t + 1) * P], kT[:, t0:t0 + m], ident[:])
                    mm.then_inc(kn_ready, 1)
                if not cur:
                    glu_start(2)
                if cur:
                    proj(c, 1, not prev)
                    pe.wait_ge(ck_landed, c * 16 + 16)
                    if prev:
                        pe.wait_ge(kn_copied, c * 2)
                    for t in range(2):
                        mm = pe.transpose(bank[:, 7, t * P:(t + 1) * P], ck[:, t, :], ident[:])
                    mm.then_inc(ckT_ready, 1)
                    bu(c, 1, False)
                    proj(c, 2, not prev)
                if prev:
                    if cur:
                        pe.wait_ge(ckT_copied, c + 1)
                    else:
                        pe.wait_ge(kn_copied, c * 2)
                    for t, (t0, m) in enumerate(TT):
                        mm = pe.transpose(bank[0:m, 7, t * P:(t + 1) * P], vT[:, t0:t0 + m], ident[:])
                    mm.then_inc(vn_ready, 1)
                if cur:
                    bu(c, 2, False)
                    if prev:
                        pe.wait_ge(y_read, c)
                    y_out(c, 0)
                if prev:
                    pe.wait_ge(wgt_ready, c)
                    pe.transpose(bank[:, 5, 0:P], wgt[:, 0:P], ident[:])
                    pe.transpose(bank[:, 5, P:2 * P], wgt[:, Z1:Z1 + P], ident[:])
                    pe.transpose(bank[:, 5, 2 * P:3 * P], wgt[:, Z1 + P:Z2], ident[:])
                    pe.transpose(bank[:, 5, 384:416], wgt[0:TS, Z2:Z2 + P], ident[0:TS, 0:TS])
                    pe.transpose(bank[:, 5, 416:448], wgt[0:TS, Z2 + P:Z2 + 2 * P], ident[0:TS, 0:TS])
                    pe.transpose(bank[0:TS, 5, 448:480], wgt[0:TS, Z2 + PAST:ZW], ident[0:TS, 0:TS]).then_inc(wT_ready, 1)
                if cur:
                    proj(c, 3, not prev)
                if not cur:
                    for m in range(4):
                        glu_rest(m)
                if prev:
                    pe.wait_ge(vn_copied, c * 2)
                    pe.wait_ge(wT_copied, c * 2)
                    pe.wait_ge(cv_landed, c * 16)
                    pe.matmul(bank[:, 6, 0:P], v_nat[:, 0, :], wT[:, 0:P], start=True, stop=True)
                    for t in range(2):
                        pe.matmul(bank[:, 6, P:TP], v_nat[:, t, :], wT[:, (1 + t) * P:(2 + t) * P], start=(t == 0), stop=(t == 1))
                    for t in range(2):
                        pe.matmul(bank[:, 6, TP:T], cv[:, t, :], wT[:, 384 + 32 * t:416 + 32 * t], start=(t == 0), stop=False)
                    pe.matmul(bank[:, 6, TP:T], v_nat[0:TS, 2, :], wT[0:TS, 448:480], start=False, stop=True).then_inc(a_ready, 1)
                if cur:
                    bu(c, 3, False)

            chunk(0, True, False, True)
            chunk(1, True, True, True)
            with pe.Fori(2, NCH) as c:
                chunk(c, True, True, False)

            GLU_AHEAD = 3

            def glu(m, k0, k1):
                s = m // 2
                w = w_ring[:, s, :].rearrange("p (k n) -> p k n", n=2 * P)
                for k in range(k0, k1):
                    mm = pe.matmul(bank[:, m % 4, 0:T], w[:, k, (m % 2) * P:(m % 2 + 1) * P], zT[:, k, :],
                                   start=(k == 0), stop=(k == NCH - 1))
                return mm

            def glu_start(m):
                pe.wait_ge(z_done, NCH - 1)
                pe.wait_ge(proj_copied, 4 * NCH)
                if m >= 2:
                    pe.wait_ge(bu_used, NJ)
                pe.wait_ge(w_landed[m // 2], 16 * (NCH + 1))
                glu(m, 0, NCH - 1)

            def glu_rest(m):
                pe.wait_ge(z_done, NCH)
                if m >= GLU_AHEAD:
                    pe.wait_ge(w_landed[m // 2], 16 * (NCH + 1))
                if m >= 4:
                    pe.wait_ge(glu_sig, m - 3)
                glu(m, 0 if m >= GLU_AHEAD else NCH - 1, NCH).then_inc(dense_done, 1)

            chunk(LAST_C, False, True, False)

            glu_rest(4)
            glu_rest(5)
            pe.wait_ge(a_copied, NCH)
            pe.wait_ge(last_ready, NJ)
            for f in range(4):
                mm = pe.transpose(bank[0:NJ, 6, f * P:(f + 1) * P], last[:, f // 2, f % 2, :], ident[:])
            mm.then_inc(lastT_ready, 1)
            pe.wait_ge(asq_ready, 1)
            pe.wait_ge(y_read, NCH)
            dense(bank[:, 4, 0:T], lambda k: ones[:], asq, NCH).then_inc(ass_ready, 1)
            glu_rest(6)
            glu_rest(7)
            pe.wait_ge(p_landed, 48)
            pe.wait_ge(ms_ready, 1)
            pe.wait_ge(last_copied, 1)
            for k in range(PLC):
                for t, (t0, m) in enumerate(TT):
                    mm = pe.transpose(bank[:, 4 if k else 6, t0:t0 + m], p_rows[0:m, t, k * P:(k + 1) * P], ident[0:m, 0:m])
                mm.then_inc(pt_ready, 1)
            pe.wait_ge(wT_copied, 2 * NCH)
            for m in range(NCH):
                pe.wait_ge(ssq_ready, m + 1)
                mm = pe.matmul(bank[:, 5, 0:T], ones[:], sq[:, m], start=(m == 0), stop=(m == NCH - 1))
            mm.then_inc(sss_ready, 1)

            def out_group(i):
                for s in range(4):
                    pe.wait_ge(w_landed[s], i * 16 + 16 * (NCH + 2))
                    pe.wait_ge(res_ready, i * 4 + (s - 3))
                    w = w_ring[:, s, :].rearrange("p (k n) -> p k n", n=P)
                    dense(bank[:, s, 0:T], lambda k: w[:, k, :], mergedT, KC).then_inc(dense_done, 1)

            pe.wait_ge(merged_a, NCH)
            pe.wait_ge(glu_sig, NCH)
            for k0, k1 in ((0, NCH), (NCH, KC)):
                for s in range(4):
                    if k0 == 0:
                        pe.wait_ge(w_landed[s], 16 * (NCH + 2))
                    else:
                        pe.wait_ge(merged_s, NCH)
                    w = w_ring[:, s, :].rearrange("p (k n) -> p k n", n=P)
                    for k in range(k0, k1):
                        mm = pe.matmul(bank[:, s, 0:T], w[:, k, :], mergedT[:, k, :], start=(k == 0), stop=(k == KC - 1))
                    if k1 == KC:
                        mm.then_inc(dense_done, 1)
            with pe.Fori(1, KC // 4) as i:
                out_group(i)
            pe.wait_ge(res_ready, KC)
            pe.wait_ge(ms_ready, 2)
            pe.wait_ge(last_copied, 1)
            for t, (t0, m) in enumerate(TT):
                if t >= 2:
                    pe.wait_ge(xh_ready, t - 1)
                for k in range(KC):
                    mm = pe.transpose(bank[0:m, 4 * (t % 2) + k // 4, (k % 4) * P:(k % 4 + 1) * P], xT[:, k, t0:t0 + m], ident[:])
                mm.then_inc(nat_ready, 1)
            for t, (t0, m) in enumerate(TT):
                pe.wait_ge(h_rows_pool, t + 1)
                pe.wait_ge(h_rows_dve, t + 1)
                pe.wait_ge(xh_ready, (2, 3, 3)[t])
                if t == 2:
                    pe.wait_ge(hT_copied, 2)
                for q in range(4):
                    for k in range(4):
                        mm = pe.transpose(hT_bank(t, q)[:, k * m:(k + 1) * m], rows[0:m, t, (4 * q + k) * P:(4 * q + k + 1) * P], ident[0:m, 0:m])
                    if t < 2:
                        mm.then_inc(hT_ready, 1)
                if t == 2:
                    mm.then_inc(hT_ready, 1)
                if t == 0:
                    pe.wait_ge(router_landed, 64)
                for k in range(KC):
                    if k % 4 == 0 and t < 2:
                        pe.wait_ge(hT_copied, 4 * t + 4 if k == 0 and t == 0 else 4 * t + k // 4 + 1)
                    elif k == 0:
                        pe.wait_ge(hT_copied, 9)
                    mm = pe.matmul(bank[0:m, 4, t * RW:(t + 1) * RW], hT[:, k, t0:t0 + m], w_router[:, k, :], start=(k == 0), stop=(k == KC - 1))
                mm.then_inc(logits_ready, 1)
            pe.wait_ge(pick_ready, 1)
            pe.matmul(bank[:, 1, 0:NE], upper[:], pick[:, 0, :], start=True, stop=True)
            pe.matmul(bank[:, 1, NE:2 * NE], ones[:], pick[:, 0, :], start=True, stop=False)
            pe.matmul(bank[:, 1, NE:2 * NE], upper[:], pick[:, 1, :], start=False, stop=True)
            for out, lhs2, m in ((bank[0:TS, 1, 2 * NE:3 * NE], upper[0:TS, 0:TS], TS), (bank[:, 1, 3 * NE:4 * NE], ones[0:TS, :], P)):
                pe.matmul(out, ones[:, 0:m], pick[:, 0, :], start=True, stop=False)
                pe.matmul(out, ones[:, 0:m], pick[:, 1, :], start=False, stop=False)
                mm = pe.matmul(out, lhs2, pick[0:TS, 2, :], start=False, stop=True)
            mm.then_inc(rank_ready, 1)

            def x_turn(b):
                pe.wait_ge(xe_landed, b * 32 + 32)
                for c in range(KC // 2):
                    mm = pe.transpose(bank[:, 1 + c // 4, (c % 4) * P:(c % 4 + 1) * P], x_exp[:, c * P:(c + 1) * P], ident[:])
                mm.then_inc(xeT_ready, 1)

            def expert(b, first, middle=None):
                pe.wait_ge(xeT_act, b + 1)
                pe.wait_ge(xeT_dve, b + 1)
                gu = bank[:, 0, :].rearrange("p (g n) -> p g n", g=2)
                for s in range(8):
                    pe.wait_ge(ew_landed[s], b * 16 + 16)
                    w = e_ring[:, s, :].rearrange("p (k f) -> p k f", k=4)
                    for kk in range(4):
                        k = 4 * (s // 2) + kk
                        for h in range(2):
                            mm = pe.matmul(gu[h * B:(h + 1) * B, s % 2, :], xT_exp[:, k % 8, k // 8, :], w[:, kk, h * FH:(h + 1) * FH],
                                           start=(s == 0 and kk == 0), stop=(k == KC - 1), skip_group_check=True)
                    mm.then_inc(ew_used, 1)
                x_turn(b + 1)
                if middle is not None:
                    middle()
                pe.wait_ge(hid_ready, b + 1)
                for c in range(2):
                    mm = pe.transpose(bank[:, 5, c * P:(c + 1) * P], hid[:, c * P:(c + 1) * P], ident[:])
                mm.then_inc(hidT_ready, 1)
                pe.wait_ge(hidT_copied, b + 1)
                if not first:
                    pe.wait_ge(ye_act, b)
                    pe.wait_ge(ye_dve, b)
                for j in range(FC):
                    pe.wait_ge(ew_landed[8 + j], b * 16 + 16)
                    for n in range(2):
                        for h in range(2):
                            mm = pe.matmul(bank[h * B:(h + 1) * B, 3 + n, :], hidT[:, j % 2, j // 2, :],
                                           e_ring[:, 8 + j, h * DH2 + n * 512:h * DH2 + (n + 1) * 512],
                                           start=(j == 0), stop=(j == FC - 1))
                    mm.then_inc(ew_used, 1)

            def ple_gate(c):
                pe.wait_ge(w_landed[0], c * 16 + 16 * (NCH + 3 + KC // 4 - EARLY_PLE))
                pe.wait_ge(ple_mul, c)
                w = w_ring[:, 0, :].rearrange("p (k n) -> p k n", n=P)
                dense(bank[:, 7, 0:T], lambda k: w[:, k, :], hT, KC).then_inc(dense_done, 1)

            def ple_proj(c):
                pe.wait_ge(w_landed[1], c * 16 + 16 * (NCH + 2 + KC // 4))
                pe.wait_ge(plg_sig, c + 1)
                w = w_ring[:, 1, 0:PLC * P].rearrange("p (k n) -> p k n", n=P)
                dense(bank[:, 7, 0:T], lambda k: w[:, k, :], pT, PLC).then_inc(dense_done, 1)

            def pair(i, first):
                expert(i * 2, first, lambda: ple_gate(i + EARLY_PLE))
                expert(i * 2 + 1, False, lambda: ple_proj(i + EARLY_PLE))

            for c in range(EARLY_PLE + 1):
                if c < EARLY_PLE:
                    slot = (0, 2)[c]
                    pe.wait_ge(w_landed[slot], 16 * (NCH + 2 + KC // 4))
                    w = w_ring[:, slot, :].rearrange("p (k n) -> p k n", n=P)
                    dense(bank[:, 7 - c, 0:T], lambda k: w[:, k, :], hT, KC).then_inc(dense_done, 1)
                if c == 0:
                    pe.wait_ge(w_landed[1], 16 * (EARLY_PLE - 1 + NCH + 2 + KC // 4))
                else:
                    pe.wait_ge(plg_sig, c)
                    w = w_ring[:, 1, (c - 1) * PLC * P:c * PLC * P].rearrange("p (k n) -> p k n", n=P)
                    dense(bank[:, 8 - c, 0:T], lambda k: w[:, k, :], pT, PLC).then_inc(dense_done, 1)
            pe.wait_ge(idx_ready, 1)
            x_turn(0)
            pair(0, True)
            with pe.Fori(1, PLE_PAIRS) as i:
                pair(i, False)
            with pe.Fori(2 * PLE_PAIRS, NE) as b:
                expert(b, False)
            count = further_blocks(pe, lambda i: expert(i + NE, False))
            pe.wait_ge(ple_done, KC)
            pe.wait_ge(ye_act, count + NE)
            pe.wait_ge(ye_dve, count + NE)

            def acc_rows(t):
                t0, m = TT[t]
                for k in range(KC):
                    pe.matmul(bank[0:m, 4 * (t % 2) + k // 4, (k % 4) * P:(k % 4 + 1) * P], accT[:, k, t0:t0 + m], ident[:],
                              start=(k % 4 == 0), stop=False, skip_group_check=True)

            acc_rows(0)
            acc_rows(1)
            pe.wait_ge(diag_ready, NT)
            for t, (t0, m) in enumerate(TT):
                if t >= 2:
                    pe.wait_ge(fin_sum, t - 1)
                    acc_rows(t)
                pe.wait_ge(y1_gathered[t], 16)
                for q in range(4):
                    mm = pe.matmul(bank[0:m, 4 * (t % 2) + q, :], gate1_diag[0:m, t, 0:m], e_ring[0:m, t, q * 512:(q + 1) * 512],
                                   start=False, stop=True, skip_group_check=True)
                mm.then_inc(fin_nat, 1)

        @block.vector
        def _(dve):
            own = OwnOrder(dve, dve_own)
            TWO_PI = 2.0 * math.pi
            PI_IN = 3.1415925
            PI_HI, ROUND = 6.28125, 12582912.0
            own(dve.memset(zero_col[:], 0.0))
            own(dve.memset(var_eps[:], 1.0))
            own(dve.memset(later, 1.0))
            own(dve.memset(tab_f[0:1, 0:SIZE + NE], 0.0))
            own(dve.memset(tab_f[0:1, SIZE + NE:SIZE + NE + 2], 2.0))

            def row_stats(t, m, src):
                for q in range(4):
                    own(dve.bn_stats(stats[0:m, t, q, :], src(q)))
                own.wait()
                own(dve.bn_aggr(mean_var[0:m, t, :], stats[0:m, t].rearrange("p q s -> p (q s)")))
                own.wait()
                return dve.tensor_scalar(var_eps[0:m, t:t + 1], mean_var[0:m, t, 1:2], LN_EPS, None, ALU.add)

            def neg_mean_of(t, m):
                return dve.scalar_tensor_tensor(out=neg_mean[0:m, t:t + 1], in0=mean_var[0:m, t, 0:1], scalar=-1.0,
                                                in1=rstd[0:m, t:t + 1], op0=ALU.mult, op1=ALU.mult)

            def f(i, j=None):
                return pr[:, i, :] if j is None else pr[:, i:j, :]

            def halves(i):
                return f(i).rearrange("j (a s) -> j a s", a=2)

            own.wait()

            def in_stats(t):
                m = TT[t][1]
                dve.wait_ge(x_landed[t], 16)
                row_stats(t, m, lambda q: rows[0:m, t, q * 512:(q + 1) * 512]).then_inc(var_ready, 1)

            in_stats(IN_ORDER[0])
            dve.wait_ge(small_landed, 80)
            dve.wait_ge(pr_act_out, 1)
            own(dve.tensor_scalar(f(0), f(0), -1e-4, None, ALU.min))
            own.wait()
            step = pr[:, 4, 2:4].unsqueeze(2).to_broadcast([NJ, 2, NS])
            own(dve.tensor_tensor(halves(5), halves(0), step, ALU.mult))
            own(dve.tensor_tensor(halves(6), halves(1), step, ALU.mult))
            own.wait()
            own(dve.tensor_scalar(f(7), f(6), 1.0 / TWO_PI, ROUND, ALU.mult, ALU.add))
            own.wait()
            own(dve.tensor_scalar(f(7), f(7), -ROUND, None, ALU.add))
            own.wait()
            own(dve.scalar_tensor_tensor(out=f(13), in0=f(7), scalar=-PI_HI, in1=f(6), op0=ALU.mult, op1=ALU.add))
            own.wait()
            own(dve.scalar_tensor_tensor(out=f(12), in0=f(7), scalar=-(TWO_PI - PI_HI), in1=f(13), op0=ALU.mult, op1=ALU.add))
            own.wait()
            own(dve.tensor_scalar(f(13), f(12), math.pi / 2, -TWO_PI, ALU.is_gt, ALU.mult))
            own.wait()
            own(dve.scalar_tensor_tensor(out=f(11), in0=f(12), scalar=math.pi / 2, in1=f(13), op0=ALU.add, op1=ALU.add))
            own.wait()
            dve.tensor_scalar(f(11, 13), f(11, 13), -PI_IN, PI_IN, ALU.max, ALU.min).then_inc(pr_act_in, 1)
            for n, t in enumerate(IN_ORDER):
                if n:
                    in_stats(t)
                dve.wait_ge(rstd_ready, n + 1)
                neg_mean_of(t, TT[t][1]).then_inc(nm_ready, 1)
            dve.wait_ge(pr_act_out, 3)
            own(dve.tensor_tensor(f(13), f(8), f(9), ALU.mult))
            own(dve.tensor_tensor(f(14), f(8), f(10), ALU.mult))
            own(dve.tensor_tensor(f(15), f(0), f(0), ALU.mult))
            own(dve.tensor_tensor(f(7), f(1), f(1), ALU.mult))
            own.wait()
            own(dve.tensor_scalar(f(13), f(13), -1.0, None, ALU.add))
            own(dve.tensor_tensor(f(15), f(15), f(7), ALU.add))
            own.wait()
            own(dve.reciprocal(f(15), f(15)))
            own(dve.tensor_tensor(f(16), f(13), f(0), ALU.mult))
            own(dve.tensor_tensor(f(17), f(14), f(1), ALU.mult))
            own(dve.tensor_tensor(f(5), f(14), f(0), ALU.mult))
            own(dve.tensor_tensor(f(6), f(13), f(1), ALU.mult))
            own.wait()
            own(dve.tensor_tensor(f(16), f(16), f(17), ALU.add))
            own(dve.tensor_tensor(f(5), f(5), f(6), ALU.subtract))
            own.wait()
            own(dve.tensor_tensor(f(16), f(16), f(15), ALU.mult))
            dve.tensor_tensor(f(17), f(5), f(15), ALU.mult).then_inc(pr_ready, 1)
            dve.wait_ge(vecT_copied, 1)
            for k in range(1, KC, 2):
                if k == KC // 2 + 3:
                    dve.wait_ge(par_copied, 1)
                    dve.wait_ge(masks_ready, 1)
                    own(dve.tensor_scalar(coef[:, :, :, 0], par[:, 3:5, :], par_b[:, 0:1], None, ALU.mult))
                    own.wait()
                    dve.tensor_scalar(coef[:, :, :, 1], par[:, 3:5, :], par_b[:, 1:2], None, ALU.mult).then_inc(coef_ready, 1)
                dve.wait_ge(xt_ready, k + 1)
                a, b = vec_at["ln_in_g"] + k, vec_at["ln_in_b"] + k
                dve.tensor_scalar(xT[:, k, :], bank[:, k % 4, 0:T], vecT[:, a:a + 1], vecT[:, b:b + 1],
                                  ALU.mult, ALU.add).then_inc(xt_odd, 1)

            def tile(c, i, first):
                n = c * JC + i
                cb = 0 if first else c % 2
                w = tb[:, ds(cb, 1), :, i, :].rearrange("p b r t -> p (b r) t")
                wre, wim = (w[:, r:r + 1, :].to_broadcast([P, 2, T]) for r in range(2))
                dve.wait_ge(bu_ready, n + 1)
                own(dve.tensor_tensor(tmp1, bank[:, 2:4, 0:T], wre, ALU.mult))
                dve.tensor_tensor(tmp2, bank[:, 2:4, 0:T], wim, ALU.mult).then_inc(bu_used, 1)
                dve.wait_ge(bu_used, n + 1)
                own(dve.tensor_tensor(rot[:, 0, :], tmp1[:, 0, :], tmp2[:, 1, :], ALU.add))
                own(dve.tensor_tensor(rot[:, 1, :], tmp1[:, 1, :], tmp2[:, 0, :], ALU.subtract))
                own.wait()
                for r in range(2):
                    for a, b, start in ((0, TP, 0.0), (TP, T, par_c[:, 5 + r, i:i + 1])):
                        own(dve.tensor_tensor_scan(scan[:, r, a:b], par_c[:, 0, i:i + 1].to_broadcast([P, b - a]),
                                                   rot[:, r, a:b], start, ALU.mult, ALU.add))
                own.wait()
                own(dve.tensor_tensor(tmp1, scan, wre, ALU.mult))
                own(dve.tensor_tensor(tmp2, scan, wim, ALU.mult))
                own.wait()
                if not first:
                    dve.wait_ge(y_part, c * 2 - 1 + i // 2)
                own(dve.tensor_tensor(h_ssm[:, i, 0, :], tmp1[:, 0, :], tmp2[:, 1, :], ALU.subtract))
                dve.tensor_tensor(h_ssm[:, i, 1, :], tmp1[:, 1, :], tmp2[:, 0, :], ALU.add).then_inc(h_ready, 1)
                dve.wait_ge(h_ready, n + 1)
                dve.tensor_copy(last[:, :, :, ds(n, 1)].rearrange("p r t j -> p r (t j)"),
                                h_ssm[:, i, :, TP - 1:T:TS]).then_inc(last_ready, 1)

            def chunk(c, cur, prev, first):
                if prev:
                    dve.wait_ge(z_ready, c)
                    own(dve.scalar_tensor_tensor(out=zm[:, 0:Z2], in0=bank[:, 5, 0:Z2], scalar=SCALE, in1=mask,
                                                 op0=ALU.mult, op1=ALU.add))
                    dve.scalar_tensor_tensor(out=zm[0:TS, Z2:ZW], in0=bank[0:TS, 6, 0:PAST + TS], scalar=SCALE,
                                             in1=mask_s[0:TS], op0=ALU.mult, op1=ALU.add).then_inc(zm_ready, 1)
                    dve.wait_ge(y_part, c * 2)
                    dve.tensor_tensor(yT, bank[:, 4, 0:T], du, ALU.add).then_inc(y_read, 1)
                    dve.wait_ge(y_read, c)
                    own(dve.tensor_tensor(y2, yT, yT, ALU.mult))
                    own.wait()
                    dve.scalar_tensor_tensor(out=y2, in0=y2, scalar=1.0 / 0.044715, in1=yT, op0=ALU.add,
                                             op1=ALU.mult).then_inc(gelu_in, 1)
                if cur:
                    own(dve.tensor_copy(par_c, par[:, :, ds(c * JC, JC)]))
                    own(dve.tensor_copy(d_c, vecT[:, ds(c + vec_at["ssm_d"], 1)]))
                    own.wait()
                    dve.wait_ge(proj_copied, c * 4 + 1)
                    dve.tensor_scalar(du, uT, d_c, None, ALU.mult).then_inc(du_ready, 1)
                    if prev:
                        dve.wait_ge(table_ready, c)
                    tile(c, 0, not prev)
                if prev:
                    dve.wait_ge(sig_ready, c)
                    if not first:
                        dve.wait_ge(wT_ready, c - 1)
                    segs = ((P, 0, P, 0), (P, Z1, TP, Z1 + 1), (TS, Z2, PAST + TS, Z2 + 2))
                    for m, z0, n, l0 in segs:
                        own(dve.tensor_tensor_scan(later[0:m, l0:l0 + n][:, ::-1], keep[0:m, z0:z0 + n][:, ::-1],
                                                   zero_col[0:m, 0:1].to_broadcast([m, n]), 1.0, ALU.mult, ALU.add))
                    own.wait()
                    for k, (m, z0, n, l0) in enumerate(segs):
                        v = dve.tensor_tensor(wgt[0:m, z0:z0 + n], sig[0:m, z0:z0 + n], later[0:m, l0 + 1:l0 + 1 + n], ALU.mult)
                        if k == 2:
                            v.then_inc(wgt_ready, 1)
                    dve.wait_ge(gelu_sig, c)
                    dve.tensor_tensor(zT[:, ds(c - 1, 1), :].rearrange("p a t -> p (a t)"), yT, ysig, ALU.mult).then_inc(z_done, 1)
                if cur:
                    for i in range(1, JC):
                        tile(c, i, not prev)

            own(table(dve, own, 0, 0, first_tp[0], first_tp[1]))
            own.wait()
            chunk(0, True, False, True)
            chunk(1, True, True, True)
            base = own.base + own.n
            with dve.Fori(2, NCH) as c:
                own.enter((c - 2) * DVE_PER_CHUNK + base)
                chunk(c, True, True, False)
                assert own.n == DVE_PER_CHUNK, own.n
            own.enter(base + (NCH - 2) * DVE_PER_CHUNK)
            chunk(LAST_C, False, True, False)

            def merge(i, n0, src, name, done):
                dve.wait_ge(rms_root, i + 1)
                r = (rms_a, rms_s)[i]
                dve.reciprocal(r, r).then_inc(rms_ready, 1)
                dve.wait_ge(rms_ready, i + 1)
                for m in range(NCH):
                    a = vec_at[name] + m
                    dve.scalar_tensor_tensor(out=mergedT[:, n0 + m, :], in0=src[:, m], scalar=vecT[:, a:a + 1],
                                             in1=r, op0=ALU.mult, op1=ALU.mult).then_inc(done, 1)

            def gated(m):
                dve.wait_ge(glu_sig, m + 1)
                dve.tensor_tensor(ssmT[:, m], zT[:, m], sg[:, m % 2], ALU.mult).then_inc(s_ready, 1)

            dve.wait_ge(z_done, NCH)
            dve.wait_ge(last_ready, NJ)
            for m in range(6):
                gated(m)
            dve.wait_ge(ass_ready, 1)
            dve.tensor_scalar(rms_a, bank[:, 4, 0:T], 1.0 / W, LN_EPS, ALU.mult, ALU.add).then_inc(ms_ready, 1)
            dve.wait_ge(a_copied, NCH)
            merge(0, 0, attnT, "g_attn", merged_a)
            gated(6)
            gated(7)
            dve.wait_ge(sss_ready, 1)
            dve.wait_ge(rms_ready, 1)
            dve.tensor_scalar(rms_s, bank[:, 5, 0:T], 1.0 / W, LN_EPS, ALU.mult, ALU.add).then_inc(ms_ready, 1)
            merge(1, NCH, ssmT, "g_ssm", merged_s)

            with dve.Fori(0, KC // 4) as i:
                for s in range(4):
                    dve.wait_ge(dense_done, i * 4 + (N_OUT + s + 1))
                    v = xT[:, ds(i * 4 + s, 1), :].rearrange("p a t -> p (a t)")
                    dve.scalar_tensor_tensor(out=v, in0=v, scalar=ALPHA, in1=bank[:, s, 0:T], op0=ALU.mult,
                                             op1=ALU.add).then_inc(res_ready, 1)

            def ln1_gain(t, m):
                dve.wait_ge(xh_ready, t + 1)
                dve.tensor_tensor(rows[0:m, t, :], rows[0:m, t, :], w_ring[0:m, 2, :], ALU.mult).then_inc(hg_ready, 1)
                dve.wait_ge(hg_ready, t + 1)
                dve.tensor_tensor(rows[0:m, t, SHARE:D], rows[0:m, t, SHARE:D], w_ring[0:m, 3, SHARE:D], ALU.add).then_inc(h_rows_dve, 1)

            own(dve.memset(logits, 0.0))
            for t, (_, m) in enumerate(TT):
                dve.wait_ge(nat_ready, t + 1)
                row_stats(t, m, lambda q: bank[0:m, 4 * (t % 2) + q, :]).then_inc(var1_ready, 1)
                dve.wait_ge(rstd1_ready, t + 1)
                neg_mean_of(t, m).then_inc(nm1_ready, 1)
                if t == 0:
                    dve.wait_ge(gb1_landed, 32)
                if t:
                    ln1_gain(t - 1, P)
            ln1_gain(NT - 1, TS)

            dve.wait_ge(logits_ready, NT)
            for t, (_, m) in enumerate(TT):
                own(dve.tensor_tensor(logits[0:m, t, :], bank[0:m, 4, t * RW:(t + 1) * RW], b_router[0:m, :], ALU.add))
            own.wait()

            def bc(v, n):
                return v.unsqueeze(2).to_broadcast([P, NT, n])

            def iob(n):
                return io[:, 0:n].unsqueeze(1).to_broadcast([P, NT, n])

            def first_max(v, n, hot, best):
                own(dve.tensor_reduce(best, v, AX_X, ALU.max))
                own.wait()
                own(dve.tensor_tensor(hot, v, bc(best, n), ALU.is_equal))
                own.wait()
                own(dve.scalar_tensor_tensor(out=hot, in0=hot, scalar=-64.0, in1=iob(n), op0=ALU.mult, op1=ALU.add))
                own.wait()
                own(dve.tensor_reduce(r_low, hot, AX_X, ALU.min))
                own.wait()
                own(dve.tensor_tensor(hot, hot, bc(r_low, n), ALU.is_equal))
                own.wait()

            gl = logits[:, :, 0:NGRP]
            first_max(gl, NGRP, g_hot, r_max)
            own(dve.tensor_tensor(d5[:, :, 0:NGRP], gl, bc(r_max, NGRP), ALU.subtract))
            own(dve.tensor_scalar(g_hot, g_hot, -1.0, -NEG, ALU.add, ALU.mult))
            own.wait()
            own(dve.tensor_tensor(el.rearrange("p t (g x) -> p t g x", g=NGRP),
                                  logits[:, :, NGRP:RW].rearrange("p t (g x) -> p t g x", g=NGRP),
                                  g_hot.unsqueeze(3).to_broadcast([P, NT, NGRP, EPG]), ALU.add))
            own.wait()
            first_max(el, NE, pick1, top1)
            own(dve.scalar_tensor_tensor(out=el, in0=pick1, scalar=NEG, in1=el, op0=ALU.mult, op1=ALU.add))
            own.wait()
            first_max(el, NE, pick2, top2)
            dve.tensor_tensor(pick, pick1, pick2, ALU.add).then_inc(pick_ready, 1)
            dve.tensor_tensor(d5[:, :, NGRP], top2, top1, ALU.subtract).then_inc(exp_in, 1)
            dve.wait_ge(exp_out, 1)
            own(dve.tensor_reduce(top1, e5[:, :, 0:NGRP], AX_X, ALU.add))
            own(dve.memset(counts, 0.0))
            own.wait()
            own(dve.scalar_tensor_tensor(out=top1, in0=e5[:, :, NGRP], scalar=1.0, in1=top1, op0=ALU.add, op1=ALU.mult))
            own.wait()
            own(dve.reciprocal(gate1[:], top1))
            own.wait()
            own(dve.tensor_tensor(gate2[:], gate1[:], e5[:, :, NGRP], ALU.mult))
            dve.wait_ge(rank_ready, 1)
            own(dve.tensor_copy(counts[:, 0:2 * NE], bank[:, 1, 0:2 * NE]))
            own(dve.tensor_copy(counts[0:TS, 2 * NE:3 * NE], bank[0:TS, 1, 2 * NE:3 * NE]))
            own(dve.tensor_copy(counts[:, 3 * NE:4 * NE], bank[:, 1, 3 * NE:4 * NE]))
            own.wait()
            cnt = counts[:, 3 * NE:4 * NE]
            zb = zero_col[:, 0:1].to_broadcast([P, NE])
            rank = counts[:, 0:3 * NE].rearrange("p (t e) -> p t e", t=NT)

            def over_tiles(v):
                return v.unsqueeze(1).to_broadcast([P, NT, NE])

            own(dve.tensor_tensor_scan(first_row, cnt, zb, 0.0, ALU.add, ALU.add))
            own(dve.tensor_scalar(more, cnt, float(B), None, ALU.is_gt))
            own.wait()
            own(dve.tensor_tensor(first_row, first_row, cnt, ALU.subtract))
            for k in range(2, MB):
                own(dve.scalar_tensor_tensor(out=more, in0=cnt, scalar=float(B * k), in1=more, op0=ALU.is_gt, op1=ALU.add))
                own.wait()
            own(dve.tensor_tensor_scan(more_at, more, zb, 0.0, ALU.add, ALU.add))
            own.wait()
            own(dve.tensor_tensor(more_at, more_at, more, ALU.subtract))
            own.wait()
            own(dve.scalar_tensor_tensor(out=jump, in0=more_at, scalar=float(NE - 1), in1=io[:], op0=ALU.add, op1=ALU.subtract))
            own(dve.tensor_tensor(place, rank, over_tiles(first_row), ALU.add))
            own.wait()

            def sum_picked(k, pk):
                own(dve.tensor_tensor(picked, pk, place, ALU.mult))
                own.wait()
                own(dve.tensor_reduce(sums[:, k, :], picked, AX_X, ALU.add))
                own.wait()

            sum_picked(0, pick1)
            sum_picked(1, pick2)
            dve.tensor_copy(idx[:, 0:2, :], sums[:, 0:2, :]).then_inc(idx_ready, 1)
            own(dve.scalar_tensor_tensor(out=place, in0=rank, scalar=float(B), in1=over_tiles(jump), op0=ALU.is_ge, op1=ALU.mult))
            own.wait()
            own(dve.tensor_tensor(place, place, over_tiles(io[:]), ALU.add))
            own.wait()
            own(dve.scalar_tensor_tensor(out=place, in0=place, scalar=float(B), in1=rank, op0=ALU.mult, op1=ALU.add))
            own.wait()
            sum_picked(2, pick1)
            sum_picked(3, pick2)
            dve.tensor_copy(idx[:, 2:4, :], sums[:, 2:4, :]).then_inc(idx_ready, 1)
            fr, mr, ma = first_row[0:1, :], more[0:1, :], more_at[0:1, :]
            o = [v.rearrange("p (i e) -> p i e", e=NE) for v in ov]
            ib = io[0:1, 0:NOV].unsqueeze(2).to_broadcast([1, NOV, NE])

            def blocks(v):
                return v.unsqueeze(1).to_broadcast([1, NOV, NE])

            j1 = jump[0:1, :]
            own(dve.tensor_tensor(o[0], blocks(ma), ib, ALU.is_le))
            own(dve.tensor_tensor(j1, ma, mr, ALU.add))
            own.wait()
            own(dve.tensor_tensor(o[1], blocks(j1), ib, ALU.is_gt))
            own(dve.tensor_copy(tab_f[0:1, NTAB + NOV:NTAB + NOV + 1], jump[0:1, NE - 1:NE]))
            own.wait()
            own(dve.tensor_tensor(o[0], o[0], o[1], ALU.mult))
            own(dve.scalar_tensor_tensor(out=j1, in0=ma, scalar=-float(B), in1=fr, op0=ALU.mult, op1=ALU.add))
            own.wait()
            own(dve.tensor_scalar(j1, j1, float(B), None, ALU.add))
            own(dve.tensor_tensor(o[1], o[0], blocks(io[0:1, :]), ALU.mult))
            own.wait()
            own(dve.tensor_tensor(o[2], o[0], blocks(j1), ALU.mult))
            own(dve.tensor_reduce(tab_f[0:1, NTAB:NTAB + NOV], o[1], AX_X, ALU.add))
            own.wait()
            own(dve.tensor_reduce(sums_ov[0:1, :], o[2], AX_X, ALU.add))
            own(dve.tensor_reduce(in_use[0:1, :], o[0], AX_X, ALU.add))
            own(dve.tensor_copy(tab_f[0:1, 0:NE], fr))
            own(dve.tensor_scalar(tab_f[0:1, SIZE:SIZE + NE], cnt[0:1, :], float(B // 2), None, ALU.is_gt))
            own.wait()
            own(dve.scalar_tensor_tensor(out=tab_f[0:1, SIZE:SIZE + NE], in0=cnt[0:1, :], scalar=float(B // 4),
                                         in1=tab_f[0:1, SIZE:SIZE + NE], op0=ALU.is_gt, op1=ALU.add))
            own.wait()
            own(dve.tensor_tensor(in_use[0:1, :], in_use[0:1, :], io[0:1, 0:NOV], ALU.mult))
            own.wait()
            own(dve.scalar_tensor_tensor(out=tab_f[0:1, NE:NE + NOV], in0=in_use[0:1, :], scalar=float(B),
                                         in1=sums_ov[0:1, :], op0=ALU.mult, op1=ALU.add))
            own.wait()
            dve.tensor_copy(tab[:], tab_f[:]).then_inc(tab_ready, 1)
            dve.wait_ge(tab_ready, 1)

            def x_copy(b):
                dve.wait_ge(xeT_ready, b + 1)
                dve.tensor_copy(xT_exp[:, 4:8].rearrange("p k h n -> p (k h n)"), bank[:, 2, :]).then_inc(xeT_dve, 1)

            def expert(b, first, middle=None):
                dve.wait_ge(gsig_ready, b + 1)
                dve.tensor_tensor(hid[:], bank[:, 0, 0:FH], sig_exp[:], ALU.mult).then_inc(gmul_ready, 1)
                dve.wait_ge(gmul_ready, b + 1)
                dve.tensor_tensor(hid[:], hid[:], bank[:, 0, FH:FE], ALU.mult).then_inc(hid_ready, 1)
                x_copy(b + 1)
                dve.wait_ge(hidT_ready, b + 1)
                dve.tensor_copy(hidT[:].rearrange("p c h n -> p (c h n)"), bank[:, 5, 0:FC * B]).then_inc(hidT_copied, 1)
                if middle is not None:
                    middle()
                dve.wait_ge(ew_used, b * NEW + NEW)
                if not first:
                    dve.wait_ge(ye_stored, b * 32)
                dve.tensor_copy(y_exp[:, 512:DH2], bank[:, 4, :]).then_inc(ye_dve, 1)

            def ple(c, bank_no=7, done=None):
                dve.wait_ge(dense_done, done or c * 2 + (N_PLE + 2))
                dve.wait_ge(plg_sig, c + 1)
                if not (done and c == 0):
                    dve.wait_ge(ple_done, c)
                dve.tensor_tensor(ple_tmp[:], ple_sig[:], bank[:, bank_no, 0:T], ALU.mult).then_inc(ple_mul, 1)
                dve.wait_ge(ple_mul, c + 1)
                v, h = (u[:, ds(c, 1), :].rearrange("p a t -> p (a t)") for u in (accT, hT))
                dve.scalar_tensor_tensor(out=v, in0=h, scalar=ALPHA, in1=ple_tmp[:], op0=ALU.mult, op1=ALU.add).then_inc(ple_done, 1)

            def pair(i, first):
                expert(i * 2, first)
                expert(i * 2 + 1, False, lambda: ple(i + EARLY_PLE))

            for c in range(EARLY_PLE):
                ple(c, 7 - c, N_PLE + EARLY_PROJ[c])
            x_copy(0)
            pair(0, True)
            with dve.Fori(1, PLE_PAIRS) as i:
                pair(i, False)
            with dve.Fori(2 * PLE_PAIRS, NE) as b:
                expert(b, False)
            further_blocks(dve, lambda i: expert(i + NE, False))

            for t, (_, m) in enumerate(TT):
                dve.tensor_scalar(gate1_diag[0:m, t, :], ident[0:m, :], gate1[0:m, t:t + 1], None, ALU.mult).then_inc(diag_ready, 1)
            dve.wait_ge(gb2_landed, 32)

            def fin_gain(t, m):
                dve.wait_ge(fin_xh, t + 1)
                dve.wait_ge(fin_g, t)
                v = y_fin[0:m, t, :]
                dve.tensor_tensor(v, v, w_ring[0:m, 2, :], ALU.mult).then_inc(fin_g, 1)

            for t, (_, m) in enumerate(TT):
                dve.wait_ge(y2_gathered[t], 16)
                dve.wait_ge(fin_nat, t + 1)
                b0 = 4 * (t % 2)
                v = y_fin[0:m, t, :]
                dve.scalar_tensor_tensor(out=v, in0=v, scalar=gate2[0:m, t:t + 1],
                                         in1=bank[0:m, b0:b0 + 4, :].rearrange("p b n -> p (b n)"),
                                         op0=ALU.mult, op1=ALU.add).then_inc(fin_sum, 1)
                dve.wait_ge(fin_sum, t + 1)
                row_stats(t, m, lambda q: y_fin[0:m, t, q * 512:(q + 1) * 512]).then_inc(fin_var, 1)
                dve.wait_ge(fin_rstd, t + 1)
                neg_mean_of(t, m).then_inc(fin_nm, 1)
                if t == 2:
                    fin_gain(1, P)
            fin_gain(NT - 1, TS)
            for t, m in ((1, P), (2, TS)):
                dve.wait_ge(fin_g, t + 1)
                v = y_fin[0:m, t, SHARE:D]
                dve.tensor_tensor(v, v, w_ring[0:m, 3, SHARE:D], ALU.add).then_inc(fin_b_dve, 1)


_INS = ['x_prompt', 'x_sample', 'p_prompt', 'p_sample', 'cache_k', 'cache_v', 'state_ssm_re', 'state_ssm_im',
        'ln_in_g', 'ln_in_b', 'w_in', 'ssm_lam_re', 'ssm_lam_im', 'ssm_log_step', 'ssm_b_re', 'ssm_b_im',
        'ssm_c_re', 'ssm_c_im', 'ssm_d', 'ssm_w_glu', 'ssm_b_glu', 'g_attn', 'g_ssm', 'w_out', 'ln1_g', 'ln1_b',
        'w_router_group', 'b_router_group', 'w_router_expert', 'b_router_expert',
        'w_exp_gate', 'w_exp_up', 'w_exp_down', 'w_ple_gate', 'w_ple_proj', 'ln2_g', 'ln2_b']
_OUTS = [(1, 256, 2048), (1, 32, 2048), (1, 1, 256, 8, 128), (1, 1, 256, 8, 128), (1, 1, 64, 64), (1, 1, 64, 64),
         (1, 1, 32, 8, 128), (1, 1, 32, 8, 128), (1, 1, 64, 64), (1, 1, 64, 64)]


def kernel(**inputs):
    import numpy as _np
    import concourse.bacc as _bacc
    from concourse import mybir as _mybir
    from concourse.bass_utils import run_bass_kernel_spmd as _run

    nc = _bacc.Bacc("TRN2", target_bir_lowering=False, num_devices=1)
    arrays, args = {}, []
    for name in _INS:
        a = _np.ascontiguousarray(inputs[name])
        arrays[f"in_{name}_dram"] = a
        args.append(nc.dram_tensor(f"in_{name}_dram", a.shape, _mybir.dt.from_np(a.dtype), kind="ExternalInput").ap())
    for i, shape in enumerate(_OUTS):
        args.append(nc.dram_tensor(f"out_{i}_dram", shape, _mybir.dt.float32, kind="ExternalOutput").ap())
    build(nc, *args)
    r = _run(nc, [arrays], core_ids=[0])
    return tuple(r.results[0][f"out_{i}_dram"] for i in range(len(_OUTS)))
```
